# Optimizing a Trainium2 kernel written in Bass

```python
import jax
import jax.numpy as jnp
from jax import lax
import numpy as np

D_MODEL = 1024
BATCH = 1
SEQ = 1024
DEPTH = 1

RET_HEADS = 4
RET_DK = 128
RET_DV = 256
GLA_HEADS = 4
GLA_DK = 128
GLA_DV = 256
GLA_GATE_RANK = 16
GLA_GATE_NORMALIZER = 16.0
CHUNK = 128
N_BRANCHES = 2
N_EXPERTS = 16
EC_CAPACITY_FACTOR = 2
D_FF = 2816
ROPE_THETA = 10000.0
NORM_EPS = 1e-6

RET_QK = RET_HEADS * RET_DK
RET_V = RET_HEADS * RET_DV
GLA_QK = GLA_HEADS * GLA_DK
GLA_V = GLA_HEADS * GLA_DV
IN_SPLITS = (RET_QK, RET_QK, RET_V, RET_V,
             GLA_QK, GLA_QK, GLA_V, GLA_V, 2 * GLA_GATE_RANK,
             N_BRANCHES * D_MODEL)
D_IN = sum(IN_SPLITS)

kernel_name = 'hybrid_retention_gla_ec_moe_encoder'

def _rmsnorm(x, gain):
    xf = x.astype(jnp.float32)
    y = xf * lax.rsqrt(jnp.mean(xf * xf, axis=-1, keepdims=True) + NORM_EPS)
    return (y * gain.astype(jnp.float32)).astype(x.dtype)

def _rope(t, positions):
    d = t.shape[-1]
    inv_freq = ROPE_THETA ** (-jnp.arange(0, d, 2, dtype=jnp.float32) / d)
    ang = positions.astype(jnp.float32)[..., None] * inv_freq
    cos = jnp.cos(ang)[:, :, None, :]
    sin = jnp.sin(ang)[:, :, None, :]
    t1, t2 = t[..., : d // 2], t[..., d // 2:]
    return jnp.concatenate([t1 * cos - t2 * sin, t2 * cos + t1 * sin], axis=-1)

def _to_chunks(t):
    b, s, h, d = t.shape
    return t.reshape(b, s // CHUNK, CHUNK, h, d).transpose(0, 3, 1, 2, 4)

def _from_chunks(t):
    b, h, n, c, d = t.shape
    return t.transpose(0, 2, 3, 1, 4).reshape(b, n * c, h, d)

def _flip(t):
    return jnp.flip(t, axis=1)

def _causal_mask(c, strict):
    pos = jnp.arange(c)
    return pos[:, None] > pos[None, :] if strict else pos[:, None] >= pos[None, :]

def _prefix_states(decay, kv):
    def step(s, inp):
        dec, u = inp
        return dec * s + u, s
    s0 = jnp.zeros_like(kv[:, :, 0])
    _, s_prev = lax.scan(step, s0, (jnp.moveaxis(decay, 2, 0), jnp.moveaxis(kv, 2, 0)))
    return jnp.moveaxis(s_prev, 0, 2)

def _retention_scan(q, k, v, log_gamma, strict):
    b, h, n, c, _ = q.shape
    pos = jnp.arange(c, dtype=jnp.float32)
    rel = pos[:, None] - pos[None, :]
    mask = _causal_mask(c, strict)
    decay_mask = jnp.where(mask, jnp.exp(jnp.where(mask, rel, 0.0) * log_gamma[:, None, None]), 0.0)
    scores = jnp.einsum('bhncd,bhnsd->bhncs', q, k) * decay_mask[None, :, None]
    intra = jnp.einsum('bhncs,bhnse->bhnce', scores, v)
    k_w = k * jnp.exp((c - 1.0 - pos)[None, :] * log_gamma[:, None])[None, :, None, :, None]
    kv = jnp.einsum('bhncd,bhnce->bhnde', k_w, v)
    chunk_decay = jnp.broadcast_to(jnp.exp(c * log_gamma)[None, :, None, None, None], (b, h, n, 1, 1))
    s_prev = _prefix_states(chunk_decay, kv)
    q_w = q * jnp.exp((pos + 1.0)[None, :] * log_gamma[:, None])[None, :, None, :, None]
    inter = jnp.einsum('bhncd,bhnde->bhnce', q_w, s_prev)
    return intra + inter

def _gla_scan(q, k, v, log_alpha, strict):
    c = q.shape[3]
    cum = jnp.cumsum(log_alpha, axis=3)
    ref = cum[:, :, :, c // 2:c // 2 + 1]
    last = cum[:, :, :, -1:]
    scores = jnp.einsum('bhncd,bhnsd->bhncs', q * jnp.exp(cum - ref), k * jnp.exp(ref - cum))
    scores = jnp.where(_causal_mask(c, strict), scores, 0.0)
    intra = jnp.einsum('bhncs,bhnse->bhnce', scores, v)
    kv = jnp.einsum('bhncd,bhnce->bhnde', k * jnp.exp(last - cum), v)
    s_prev = _prefix_states(jnp.swapaxes(jnp.exp(last), -1, -2), kv)
    inter = jnp.einsum('bhncd,bhnde->bhnce', q * jnp.exp(cum), s_prev)
    return intra + inter

def _mixer(h, positions, w_in, ret_decay_fwd, ret_decay_bwd, ret_norm,
           gla_gate_w_fwd, gla_gate_b_fwd, gla_gate_w_bwd, gla_gate_b_bwd, gla_norm,
           w_branch_ret, w_branch_gla, w_out):
    b, s, _ = h.shape
    f32 = jnp.float32
    proj = h @ w_in
    split_at = [int(i) for i in np.cumsum(IN_SPLITS)[:-1]]
    rq, rk, rv, rg, gq, gk, gv, gr, ga, gate_logits = jnp.split(proj, split_at, axis=-1)

    rq = _rope(rq.astype(f32).reshape(b, s, RET_HEADS, RET_DK), positions) * RET_DK ** -0.5
    rk = _rope(rk.astype(f32).reshape(b, s, RET_HEADS, RET_DK), positions)
    rv = rv.astype(f32).reshape(b, s, RET_HEADS, RET_DV)
    lg_f = jax.nn.log_sigmoid(ret_decay_fwd.astype(f32))
    lg_b = jax.nn.log_sigmoid(ret_decay_bwd.astype(f32))
    ret = _from_chunks(_retention_scan(_to_chunks(rq), _to_chunks(rk), _to_chunks(rv), lg_f, False))
    ret = ret + _flip(_from_chunks(_retention_scan(
        _to_chunks(_flip(rq)), _to_chunks(_flip(rk)), _to_chunks(_flip(rv)), lg_b, True)))
    mu = jnp.mean(ret, axis=-1, keepdims=True)
    var = jnp.mean(jnp.square(ret - mu), axis=-1, keepdims=True)
    ret = ((ret - mu) * lax.rsqrt(var + NORM_EPS)).reshape(b, s, RET_V) * ret_norm.astype(f32)
    ret = (ret * jax.nn.silu(rg.astype(f32))).astype(h.dtype)

    gq = gq.astype(f32).reshape(b, s, GLA_HEADS, GLA_DK) * GLA_DK ** -0.5
    gk = gk.astype(f32).reshape(b, s, GLA_HEADS, GLA_DK)
    gv = gv.astype(f32).reshape(b, s, GLA_HEADS, GLA_DV)
    ga_f, ga_b = jnp.split(ga.astype(f32), 2, axis=-1)
    la_f = (jax.nn.log_sigmoid(ga_f @ gla_gate_w_fwd.astype(f32) + gla_gate_b_fwd.astype(f32))
            / GLA_GATE_NORMALIZER).reshape(b, s, GLA_HEADS, GLA_DK)
    la_b = (jax.nn.log_sigmoid(ga_b @ gla_gate_w_bwd.astype(f32) + gla_gate_b_bwd.astype(f32))
            / GLA_GATE_NORMALIZER).reshape(b, s, GLA_HEADS, GLA_DK)
    gla = _from_chunks(_gla_scan(_to_chunks(gq), _to_chunks(gk), _to_chunks(gv), _to_chunks(la_f), False))
    gla = gla + _flip(_from_chunks(_gla_scan(
        _to_chunks(_flip(gq)), _to_chunks(_flip(gk)), _to_chunks(_flip(gv)), _to_chunks(_flip(la_b)), True)))
    gla = gla * lax.rsqrt(jnp.mean(gla * gla, axis=-1, keepdims=True) + NORM_EPS)
    gla = gla.reshape(b, s, GLA_V) * gla_norm.astype(f32)
    gla = (gla * jax.nn.silu(gr.astype(f32))).astype(h.dtype)

    g_ret, g_gla = jnp.split(jax.nn.sigmoid(gate_logits.astype(f32)), N_BRANCHES, axis=-1)
    merged = g_ret * (ret @ w_branch_ret).astype(f32) + g_gla * (gla @ w_branch_gla).astype(f32)
    return merged.astype(h.dtype) @ w_out

def _expert_choice_moe(h, w_router, w_gate, w_up, w_down):
    b, s, d = h.shape
    capacity = EC_CAPACITY_FACTOR * s // N_EXPERTS
    affinity = jax.nn.softmax((h @ w_router).astype(jnp.float32), axis=-1)
    gate, idx = lax.top_k(jnp.swapaxes(affinity, 1, 2), capacity)
    xg = jax.vmap(lambda hb, ib: hb[ib])(h, idx)
    act = jax.nn.silu(jnp.einsum('becd,edf->becf', xg, w_gate)) * jnp.einsum('becd,edf->becf', xg, w_up)
    y = jnp.einsum('becf,efd->becd', act, w_down) * gate[..., None].astype(h.dtype)
    return jax.vmap(lambda ib, yb: jnp.zeros((s, d), yb.dtype).at[ib.reshape(-1)].add(yb.reshape(-1, d)))(idx, y)

def setup_inputs(seed: int = 0) -> dict:
    key = jax.random.key(seed)
    ks = jax.random.split(key, 24)
    L, D = DEPTH, D_MODEL
    f32 = jnp.float32

    def dense(k, shape, fan_in):
        return jax.random.normal(k, shape, f32) * fan_in ** -0.5

    def gain(k, shape):
        return 1.0 + 0.02 * jax.random.normal(k, shape, f32)

    gamma0 = 1.0 - 2.0 ** (-5.0 - np.arange(RET_HEADS))
    logit0 = jnp.asarray(np.log(gamma0) - np.log1p(-gamma0), f32)
    return {
        'x': jax.random.normal(ks[0], (BATCH, SEQ, D), f32),
        'positions': jnp.broadcast_to(jnp.arange(SEQ, dtype=jnp.int32), (BATCH, SEQ)),
        'norm_mix': gain(ks[1], (L, D)),
        'w_in': dense(ks[2], (L, D, D_IN), D),
        'ret_decay_fwd': logit0 + 0.05 * jax.random.normal(ks[3], (L, RET_HEADS), f32),
        'ret_decay_bwd': logit0 + 0.05 * jax.random.normal(ks[4], (L, RET_HEADS), f32),
        'ret_norm': gain(ks[5], (L, RET_V)),
        'gla_gate_w_fwd': dense(ks[6], (L, GLA_GATE_RANK, GLA_QK), GLA_GATE_RANK),
        'gla_gate_b_fwd': 0.1 * jax.random.normal(ks[7], (L, GLA_QK), f32),
        'gla_gate_w_bwd': dense(ks[8], (L, GLA_GATE_RANK, GLA_QK), GLA_GATE_RANK),
        'gla_gate_b_bwd': 0.1 * jax.random.normal(ks[9], (L, GLA_QK), f32),
        'gla_norm': gain(ks[10], (L, GLA_V)),
        'w_branch_ret': dense(ks[11], (L, RET_V, D), RET_V),
        'w_branch_gla': dense(ks[12], (L, GLA_V, D), GLA_V),
        'w_out': dense(ks[13], (L, D, D), D),
        'norm_ffn': gain(ks[14], (L, D)),
        'w_router': dense(ks[15], (L, D, N_EXPERTS), D),
        'w_gate': dense(ks[16], (L, N_EXPERTS, D, D_FF), D),
        'w_up': dense(ks[17], (L, N_EXPERTS, D, D_FF), D),
        'w_down': dense(ks[18], (L, N_EXPERTS, D_FF, D), D_FF),
        'norm_final': gain(ks[19], (D,)),
    }

def reference(x, positions, norm_mix, w_in, ret_decay_fwd, ret_decay_bwd, ret_norm,
              gla_gate_w_fwd, gla_gate_b_fwd, gla_gate_w_bwd, gla_gate_b_bwd, gla_norm,
              w_branch_ret, w_branch_gla, w_out, norm_ffn, w_router, w_gate, w_up, w_down,
              norm_final):
    for l in range(DEPTH):
        h = _rmsnorm(x, norm_mix[l])
        x = x + _mixer(h, positions, w_in[l], ret_decay_fwd[l], ret_decay_bwd[l], ret_norm[l],
                       gla_gate_w_fwd[l], gla_gate_b_fwd[l], gla_gate_w_bwd[l], gla_gate_b_bwd[l],
                       gla_norm[l], w_branch_ret[l], w_branch_gla[l], w_out[l])
        h = _rmsnorm(x, norm_ffn[l])
        x = x + _expert_choice_moe(h, w_router[l], w_gate[l], w_up[l], w_down[l])
    return _rmsnorm(x, norm_final)


_drawn_inputs = setup_inputs


def setup_inputs(seed=0):
    import zlib

    import numpy as np

    out = dict(_drawn_inputs(seed))
    spreads = {}
    factors = {'ret_norm': 5.868,
     'gla_gate_b_fwd': 4.179,
     'gla_gate_b_bwd': 4.279,
     'gla_norm': 6.069,
     'norm_ffn': 3.961,
     'norm_final': 2.833}
    for name, (base, spread) in spreads.items():
        noise = np.random.default_rng([zlib.crc32(name.encode()), seed]).standard_normal(out[name].shape)
        drawn = base * np.exp(spread * noise) if base else spread * noise
        out[name] = jnp.asarray(drawn.astype(out[name].dtype))
    for name, factor in factors.items():
        out[name] = (out[name] * factor).astype(out[name].dtype)
    return out
```

```python
from contextlib import ExitStack

import numpy as np

import concourse.bass as bass
from concourse import mybir

ALU = mybir.AluOpType
ACT = mybir.ActivationFunctionType
F32 = mybir.dt.float32
F32R = mybir.dt.float32r
I32 = mybir.dt.int32
U32 = mybir.dt.uint32
AX_X = mybir.AxisListType.X

P = 128
SEQ = 1024
D = 1024
NT = SEQ // P
KC = D // P
HEADS = 4
DK = 128
DV = 256
RANK = 16
EXPERTS = 16
D_FF = 2816
CAPACITY = 2 * SEQ // EXPERTS
EPS = 1e-6
QK_SCALE = DK ** -0.5
GATE_NORMALIZER = 16.0
COLS = 256

RET_Q, RET_K, RET_V, RET_G = 0, 512, 1024, 2048
GLA_Q, GLA_K, GLA_V, GLA_G = 3072, 3584, 4096, 5120
GATE_A, GATE_LOGITS = 6144, 6176

C_IDENT, C_ROT, C_AHEAD, C_BEHIND = 0, 128, 256, 384
C_ROW, C_UPTO, C_FROM, C_AFTER = 512, 768, 896, 1024
C_INV_FREQ, C_COL, C_EPS, C_CHUNK = 1152, 1153, 1155, 1156
N_CONST = 1160


def make_constants():
    c = np.zeros((P, N_CONST), np.float32)
    j, i = np.arange(P)[:, None], np.arange(P)[None, :]
    c[:, C_IDENT:C_IDENT + P] = i == j
    half = DK // 2
    c[:, C_ROT:C_ROT + P] = np.where(j == i + half, -1.0, 0.0) + np.where(j == i - half, 1.0, 0.0)
    c[:, C_AHEAD:C_AHEAD + P] = np.maximum(i - j, 0)
    c[:, C_BEHIND:C_BEHIND + P] = np.maximum(j - i, 0)
    c[:, C_ROW:C_ROW + P] = i + 1
    c[:, C_ROW + P:C_ROW + 2 * P] = P - i
    c[:, C_UPTO:C_UPTO + P] = j <= i
    c[:, C_FROM:C_FROM + P] = j >= i
    c[:, C_AFTER:C_AFTER + P] = j > i
    freq = np.float32(10000.0) ** (-np.arange(0, DK, 2, dtype=np.float32) / np.float32(DK))
    c[:, C_INV_FREQ] = np.tile(freq, 2)
    c[:, C_COL] = P - 1 - np.arange(P)
    c[:, C_COL + 1] = np.arange(P)
    c[:, C_EPS] = EPS
    c[:, C_CHUNK] = P
    return c


class Chain:

    def __init__(self, eng, sem):
        self.eng, self.sem, self.base, self.n = eng, sem, 0, 0

    def start(self, base=0):
        self.base, self.n = base, 0

    def mark(self, ins):
        self.n += 1
        ins.then_inc(self.sem, 1)

    def wait(self):
        self.eng.wait_ge(self.sem, self.base + self.n)

    def link(self, ins):
        self.mark(ins)
        self.wait()


def inverse_root(nc, chain, out, root, square, scratch):
    chain.link(nc.vector.reciprocal(out, root))
    chain.link(nc.vector.tensor_tensor(scratch, out, out, ALU.mult))
    chain.link(nc.vector.tensor_tensor(scratch, scratch, square, ALU.mult))
    chain.link(nc.vector.tensor_scalar(scratch, scratch, -0.5, 1.5, ALU.mult, ALU.add))
    chain.link(nc.vector.tensor_tensor(out, out, scratch, ALU.mult))


def product(nc, out, x, w, x_at, w_at, chunks=KC, start=True, stop=True):
    for kc in range(chunks):
        for xi, wi in ((0, 0), (0, 1), (1, 0)):
            last = nc.tensor.matmul(out, x_at(x[xi], kc), w_at(w[wi], kc),
                                    start=start and kc == 0 and (xi, wi) == (0, 0),
                                    stop=stop and kc == chunks - 1 and (xi, wi) == (1, 0))
    return last


def normalize_input(nc, sems, x_in, x, norm_mix, consts, cst, hT):
    with ExitStack() as ctx:
        sb = lambda n, s, d=F32: ctx.enter_context(nc.sbuf_tensor(n, s, d))
        sem = lambda n: sems.enter_context(nc.semaphore(n))
        x_sb = sb("n1_x", [P, NT, D])
        xn = sb("n1_xn", [P, NT, D])
        gain = sb("n1_gain", [P, KC])
        stat = sb("n1_stat", [P, 5, NT])
        val = sb("n1_val", [P, 2, 4, P])
        tp = [ctx.enter_context(nc.psum_tensor(f"n1_tp{b}", [P, 4, P], F32)) for b in range(2)]
        small_in = sem("n1_small_in")
        squared = sem("n1_squared")
        rooted = sem("n1_rooted")
        meaned = sem("n1_meaned")
        dve_chain = sem("n1_dve_chain")
        normed = sem("n1_normed")
        transposed = sem("n1_transposed")
        scaled = sem("n1_scaled")
        high = sem("n1_high")
        low = sem("n1_low")
        ident = cst[:, C_IDENT:C_IDENT + P]
        with nc.Block() as block:
            @block.sync
            def _(sp):
                sp.dma_start(x_sb[:, 0, :], x[0, 0:P, :]).then_inc(x_in[0], 16)
                sp.dma_start(cst[:], consts).then_inc(small_in, 16)
                sp.dma_start(gain[:], norm_mix).then_inc(small_in, 16)
                for t in range(1, NT):
                    sp.dma_start(x_sb[:, t, :], x[0, t * P:(t + 1) * P, :]).then_inc(x_in[t], 16)

            @block.scalar
            def _(act):
                def split_high(u):
                    act.wait_ge(scaled, u + 1)
                    t, c0 = u // 2, 4 * (u % 2)
                    nc.scalar.activation(hT[0][:, c0:c0 + 4, t * P:(t + 1) * P], val[:, u % 2],
                                         ACT.Copy).then_inc(high, 1)

                act.wait_ge(small_in, 32)
                for t in range(NT):
                    act.wait_ge(x_in[t], 16)
                    nc.scalar.activation(xn[:, t, :], x_sb[:, t, :], ACT.Square,
                                         accum_out=stat[:, 0, t:t + 1]).then_inc(squared, 1)
                    act.wait_ge(meaned, t + 1)
                    nc.scalar.activation(stat[:, 1, t:t + 1], stat[:, 3, t:t + 1], ACT.Sqrt).then_inc(rooted, 1)
                    for half in range(2) if t else ():
                        split_high(2 * (t - 1) + half)
                for half in range(2):
                    split_high(2 * (NT - 1) + half)

            @block.vector
            def _(dve):
                def split_low(u):
                    t, c0 = u // 2, 4 * (u % 2)
                    at = (slice(None), slice(c0, c0 + 4), slice(t * P, (t + 1) * P))
                    dve.wait_ge(high, u + 1)
                    nc.vector.tensor_tensor(hT[1][at], val[:, u % 2], hT[0][at], ALU.subtract).then_inc(low, 1)

                def scale(u):
                    c0 = 4 * (u % 2)
                    dve.wait_ge(transposed, u + 1)
                    if u >= 2:
                        dve.wait_ge(low, u - 1)
                    nc.vector.tensor_tensor(val[:, u % 2], tp[u % 2][:],
                                            gain[:, c0:c0 + 4].unsqueeze(2).to_broadcast([P, 4, P]),
                                            ALU.mult).then_inc(scaled, 1)

                chain = Chain(dve, dve_chain)
                dve.wait_ge(small_in, 32)
                for t in range(NT + 1):
                    if t < NT:
                        dve.wait_ge(squared, t + 1)
                        nc.vector.tensor_scalar(stat[:, 3, t:t + 1], stat[:, 0, t:t + 1], 1.0 / D, EPS,
                                                ALU.mult, ALU.add).then_inc(meaned, 1)
                        dve.wait_ge(rooted, t + 1)
                        inverse_root(nc, chain, stat[:, 2, t:t + 1], stat[:, 1, t:t + 1],
                                     stat[:, 3, t:t + 1], stat[:, 4, t:t + 1])
                        nc.vector.tensor_scalar(xn[:, t, :], x_sb[:, t, :], stat[:, 2, t:t + 1], None,
                                                ALU.mult).then_inc(normed, 1)
                    if t:
                        for u in (2 * t - 2, 2 * t - 1):
                            scale(u)
                        for u in (2 * t - 2, 2 * t - 1):
                            split_low(u)

            @block.tensor
            def _(pe):
                pe.wait_ge(small_in, 32)
                for u in range(2 * NT):
                    t = u // 2
                    pe.wait_ge(normed, t + 1)
                    if u >= 2:
                        pe.wait_ge(scaled, u - 1)
                    for c in range(4):
                        kc = 4 * (u % 2) + c
                        last = nc.tensor.transpose(tp[u % 2][:, c, :], xn[:, t, kc * P:(kc + 1) * P], ident)
                    last.then_inc(transposed, 1)


def heads(nc, sems, branch, w_in, decay, gain_cols, positions, gate_w, gate_b, cst, hT, out_T, gates):
    ret = branch == "ret"
    q0, k0, v0, g0 = (RET_Q, RET_K, RET_V, RET_G) if ret else (GLA_Q, GLA_K, GLA_V, GLA_G)
    m0 = GATE_LOGITS + (0 if ret else D)
    m_out = 0 if ret else D
    kinds = (("turn", 4), ("keys", 2), ("state", NT - 1), ("score", 2), ("flip", 4)) if ret else \
        (("gate", 4), ("cum", 4), ("keys", 4), ("state", NT - 1), ("score", 4), ("flip", 4))
    units = [(kind, i) for kind, n in kinds for i in range(n)]
    order = {u: n for n, u in enumerate(units)}
    n_units = len(units)
    uses = ((n_units + 1) // 2, n_units // 2)
    A, B, C, DD = 0, 1, 2, 3
    T_LOAD = (32, 16, 16, 16)
    n_chain = 6 + 4 + NT * 2 if ret else 0

    with ExitStack() as ctx:
        sb = lambda n, s, d=F32: ctx.enter_context(nc.sbuf_tensor(f"{branch}_{n}", s, d))
        sem = lambda n: sems.enter_context(nc.semaphore(f"{branch}_{n}"))
        psum = lambda n, s: ctx.enter_context(nc.psum_tensor(f"{branch}_{n}", s, F32))
        w_raw = sb("w_raw", [P, KC, COLS])
        w_part = [[sb(f"w_part{i}{k}", [P, KC, COLS], F32R) for k in range(2)] for i in range(2)]
        qk_raw = sb("qk_raw", [P, 2, SEQ])
        o_n = qk_raw[:].rearrange("p w n -> p (w n)").rearrange("p (n e) -> p n e", e=DV)
        v_sb = sb("v", [P, NT, DV])
        g_sb = sb("g", [P, NT, DV])
        curve = sb("curve", [P, 2, SEQ])
        tmp = sb("tmp", [P, 2, SEQ])
        tmp_flat = tmp[:].rearrange("p w n -> p (w n)")
        n_dir = 1 if ret else 2
        qd = sb("qd", [P, n_dir, SEQ])
        kd = sb("kd", [P, n_dir, SEQ])
        qw = sb("qw", [P, 2, SEQ])
        kw = sb("kw", [P, NT, 2, DK])
        kw_flat = kw[:].rearrange("p n w d -> p (n w d)")
        states = sb("states", [P, 2, NT - 1, DV])
        probs = sb("probs", [P, NT, P])
        m_stage = sb("m_stage", [P, 2, 2, COLS])
        stats = sb("stats", [P, NT, 6])
        mv = sb("mv", [P, NT, 2])
        small = sb("small", [P, 4, NT])
        gain = sb("gain", [P, KC])
        head_cols = sb("head_cols", [P, 4])
        dec = sb("dec", [P, 2, HEADS if ret else NT])
        proj = [psum(f"proj{b}", [P, 512]) for b in range(2)]
        work = [psum(f"work{b}", [P, 512]) for b in range(2)]
        out = psum("out", [P, NT, DV])

        w_loaded = sem("w_loaded")
        w_high = sem("w_high")
        w_split = sem("w_split")
        proj_done = sem("proj_done")
        proj_taken = sem("proj_taken")
        work_done = sem("work_done")
        work_taken = [sem(f"work_taken{b}") for b in range(2)]
        roped = sem("roped")
        q_weighted = sem("q_weighted")
        state_f = sem("state_f")
        out_done = sem("out_done")
        squares_done = sem("squares_done")
        rooted = sem("rooted")
        out_normed = sem("out_normed")
        out_gated = sem("out_gated")
        stage_stored = sem("stage_stored")
        stage_free = sem("stage_free")
        m_stored = sem("m_stored")
        m_free = sem("m_free")
        dve_chain = sem("dve_chain")
        act_chain = sem("act_chain")
        small_in = sem("small_in")
        ident = cst[:, C_IDENT:C_IDENT + P]

        if ret:
            pos_i = sb("pos_i", [P, SEQ], I32)
            rows = sb("rows", [P, HEADS, 2, P])
            dists = sb("dists", [P, HEADS, P])
            cols = sb("cols", [P, HEADS, 2])
            lg = sb("lg", [P, 2, HEADS])
            lt = sb("lt", [P, 4, 2, HEADS])
            angles_done = sem("angles_done")
            tables_done = sem("tables_done")
            act_tables = sem("act_tables")
        else:
            low_rank = sb("low_rank", [64, SEQ])
            gate_all = cst[0:64, C_ROT:C_ROT + HEADS * DK]
            gate_head = sb("gate_head", [64, DK])
            wa_raw = states[:, 0, 0, :].rearrange("p (c n) -> p c n", c=KC)
            low_done = sem("low_done")
            low_taken = sem("low_taken")
            ones_set = sem("ones_set")
            gate_ready = sem("gate_ready")
            z_folded = sem("z_folded")
            decay_logs = sem("decay_logs")
            decays_ready = sem("decays_ready")
            diff_done = sem("diff_done")
            exp_done = sem("exp_done")
            keys_weighted = sem("keys_weighted")

        def taken_after(h, kind, i):
            n = order[(kind, i)]
            return n % 2, uses[n % 2] * h + n // 2 + 2

        def wait_taken(eng, h, kind, i):
            b, count = taken_after(h, kind, i)
            eng.wait_ge(work_taken[b], count)

        def wait_work(eng, h, kind, i):
            eng.wait_ge(work_done, n_units * h + order[(kind, i)] + 1)

        def bank(kind, i):
            return work[order[(kind, i)] % 2]

        def took(ins, kind, i):
            ins.then_inc(work_taken[order[(kind, i)] % 2], 1)

        def proj_unit(tile, i):
            return 4 * tile + i

        def wait_proj(eng, h, tile, i):
            eng.wait_ge(proj_done, 16 * h + proj_unit(tile, i) + 1)

        block = ctx.enter_context(nc.Block())

        @block.sync
        def _(sp):
            w = w_in[0].rearrange("(c p) n -> p c n", p=P)

            def load(tile, h):
                if tile == A:
                    sp.dma_start(w_raw[:, :, 0:DK], w[:, :, bass.ds(h * DK + q0, DK)]).then_inc(w_loaded, 16)
                    sp.dma_start(w_raw[:, :, DK:2 * DK], w[:, :, bass.ds(h * DK + k0, DK)]).then_inc(w_loaded, 16)
                else:
                    c0 = {B: v0, C: g0, DD: m0}[tile]
                    sp.dma_start(w_raw[:], w[:, :, bass.ds(h * COLS + c0, COLS)]).then_inc(w_loaded, 16)

            load(A, 0)
            sp.dma_start(gain[:], gain_cols).then_inc(small_in, 16)
            if ret:
                sp.dma_start(pos_i[:], positions[0:1, :].partition_broadcast(P) if False else
                             positions.to_broadcast([P, SEQ])).then_inc(small_in, 16)
                for k in range(2):
                    sp.dma_start(lg[:, k, :], decay[k].to_broadcast([P, HEADS])).then_inc(small_in, 16)
            else:
                with nc.allow_non_contiguous_dma(reason="128-byte rows"):
                    sp.dma_start(wa_raw, w[:, :, GATE_A:GATE_A + 2 * RANK]).then_inc(small_in, 16)
                for k in range(2):
                    sp.dma_start(gate_all[32 * k:32 * k + RANK, :], gate_w[k][0]).then_inc(small_in, 16)
                    sp.dma_start(gate_all[32 * k + RANK:32 * k + RANK + 1, :], gate_b[k]).then_inc(small_in, 16)
            with sp.Fori(0, HEADS) as h:
                for n, tile in enumerate((B, C, DD, A)):
                    sp.wait_ge(w_split, 4 * h + n + 1)
                    load(tile, h + 1 if tile == A else h)

        @block.gpsimd
        def _(pool):
            pool.sem_inc(stage_free, 1)
            pool.sem_inc(m_free, 2)
            with pool.Fori(0, HEADS) as h:
                def store_gates(i):
                    pool.wait_ge(proj_taken, 16 * h + proj_unit(DD, i) + 1 + 2)
                    pool.dma_start(gates.rearrange("(t p) n -> p t n", p=P)[
                        :, 2 * i:2 * i + 2, bass.ds(h * COLS + m_out, COLS)], m_stage[:, i % 2]
                        ).then_inc(m_stored, 16)
                    pool.wait_ge(m_stored, 64 * h + 16 * (i + 1))
                    pool.sem_inc(m_free, 1)
                for i in range(4):
                    store_gates(i)
                for i in range(4):
                    wait_taken(pool, h, "flip", i)
                    pool.dma_start(out_T[bass.ds(2 * h + i % 2, 1), :, (i // 2) * 512:(i // 2) * 512 + 512]
                                   .rearrange("a p n -> p (a n)"),
                                   tmp_flat[:, i * 512:(i + 1) * 512]).then_inc(stage_stored, 16)
                pool.wait_ge(stage_stored, 64 * h + 64)
                pool.sem_inc(stage_free, 1)

        @block.scalar
        def _(act):
            act.sem_inc(proj_taken, 2)
            for b in range(2):
                act.sem_inc(work_taken[b], 1)
            chain = Chain(act, act_chain)

            def split_high(n, tile, at, loaded):
                act.wait_ge(w_loaded, loaded)
                nc.scalar.activation(w_part[at][0][:], w_raw[:], ACT.Copy).then_inc(w_high, 1)

            split_high(0, A, 0, 32)
            if ret:
                act.wait_ge(small_in, 64)
                chain.link(nc.scalar.activation(lt[:, 0], lg[:], ACT.Abs))
                chain.link(nc.scalar.activation(lt[:, 0], lt[:, 0], ACT.Exp, scale=-1.0))
                nc.scalar.activation(lt[:, 0], lt[:, 0], ACT.Ln, bias=1.0).then_inc(act_tables, 1)
                act.wait_ge(tables_done, 1)
                for h in range(HEADS):
                    for k in range(2):
                        s = lt[:, 3, k, h:h + 1]
                        nc.scalar.activation(rows[:, h, k, :], cst[:, C_ROW + k * P:C_ROW + (k + 1) * P],
                                             ACT.Exp, scale=s)
                        nc.scalar.activation(cols[:, h, k:k + 1], cst[:, C_COL + k:C_COL + k + 1],
                                             ACT.Exp, scale=s)
                        nc.scalar.activation(dec[:, k, h:h + 1], cst[:, C_CHUNK:C_CHUNK + 1],
                                             ACT.Exp, scale=s)
                nc.scalar.activation(dists[:], dists[:], ACT.Exp).then_inc(act_tables, 1)
                act.wait_ge(angles_done, 1)
                nc.scalar.activation(curve[:], curve[:], ACT.Sin).then_inc(act_tables, 1)
            else:
                act.wait_ge(ones_set, 1)
                for u in range(4):
                    k, half = u // 2, u % 2
                    act.wait_ge(low_done, u + 1)
                    nc.scalar.activation(low_rank[32 * k:32 * k + RANK, half * 512:half * 512 + 512],
                                         proj[u % 2][32 * k:32 * k + RANK, :], ACT.Copy).then_inc(low_taken, 1)
                act.wait_ge(small_in, 96)

            chain_base = chain.n
            with act.Fori(0, HEADS) as h:
                n_act = 0 if ret else 2
                chain.start(chain_base + n_act * h)
                loaded = 32 + sum(T_LOAD) * h

                def split_next(tile):
                    n = (tile + 1) % 4
                    count = loaded + sum((T_LOAD[B], T_LOAD[C], T_LOAD[DD], T_LOAD[A])[:tile + 1])
                    act.wait_ge(w_loaded, count)
                    nc.scalar.activation(w_part[n % 2][0][:], w_raw[:], ACT.Copy).then_inc(w_high, 1)

                def evacuate(tile, i):
                    wait_proj(act, h, tile, i)
                    src = proj[i % 2][:]
                    if tile == A:
                        ins = nc.scalar.activation(qk_raw[:, i // 2, (i % 2) * 512:(i % 2) * 512 + 512], src,
                                                   ACT.Copy, scale=QK_SCALE if i < 2 else 1.0)
                    elif tile == B:
                        ins = nc.scalar.activation(v_sb[:, 2 * i:2 * i + 2, :],
                                                   src.rearrange("p (t n) -> p t n", t=2), ACT.Copy)
                    elif tile == C:
                        ins = nc.scalar.activation(g_sb[:, 2 * i:2 * i + 2, :],
                                                   src.rearrange("p (t n) -> p t n", t=2), ACT.Silu)
                    else:
                        act.wait_ge(m_free, 4 * h + i + 1)
                        ins = nc.scalar.activation(m_stage[:, i % 2],
                                                   src.rearrange("p (t n) -> p t n", t=2), ACT.Sigmoid)
                    ins.then_inc(proj_taken, 1)

                if not ret:
                    nc.scalar.activation(gate_head[0:RANK + 1, :], gate_all[0:RANK + 1, bass.ds(h * DK, DK)], ACT.Copy)
                    nc.scalar.activation(gate_head[32:32 + RANK + 1, :],
                                         gate_all[32:32 + RANK + 1, bass.ds(h * DK, DK)],
                                         ACT.Copy).then_inc(gate_ready, 1)
                evacuate(A, 0)
                split_next(A)
                for i in range(1, 4):
                    evacuate(A, i)
                if not ret:
                    act.wait_ge(stage_free, h + 1)
                    for i in range(4):
                        wait_work(act, h, "gate", i)
                        nc.scalar.activation(tmp_flat[:, i * 512:i * 512 + 512], bank("gate", i)[:],
                                             ACT.Abs).then_inc(z_folded, 1)
                    act.wait_ge(z_folded, 4 * h + 4)
                    chain.link(nc.scalar.activation(tmp_flat, tmp_flat, ACT.Exp, scale=-1.0))
                    chain.link(nc.scalar.activation(tmp_flat, tmp_flat, ACT.Ln, bias=1.0))
                evacuate(B, 0)
                split_next(B)
                for i in range(1, 4):
                    evacuate(B, i)
                if not ret:
                    for i in range(4):
                        wait_work(act, h, "cum", i)
                        took(nc.scalar.activation(curve[:, i // 2, (i % 2) * 512:(i % 2) * 512 + 512],
                                                  bank("cum", i)[:], ACT.Copy), "cum", i)
                evacuate(C, 0)
                nc.scalar.activation(head_cols[:, 0:2], gain[:, bass.ds(2 * h, 2)], ACT.Copy)
                if ret:
                    nc.scalar.activation(head_cols[:, 2:4], cols[:, bass.ds(h, 1), :].rearrange("p h k -> p (h k)"),
                                         ACT.Copy)
                split_next(C)
                if not ret:
                    for k in range(2):
                        act.wait_ge(diff_done, 4 * h + k + 1)
                        nc.scalar.activation(qd[:, k, :], tmp[:, k, :], ACT.Exp)
                        nc.scalar.activation(kd[:, k, :], tmp[:, k, :], ACT.Exp, scale=-1.0).then_inc(exp_done, 1)
                    evacuate(C, 1)
                    for k in range(2):
                        nc.scalar.activation(qw[:, k, :], curve[:, k, :], ACT.Exp)
                        last = P - 1 if k == 0 else 0
                        nc.scalar.activation(dec[:, k, :], curve[:, k, :].rearrange("p (n i) -> p n i", i=P)[:, :, last],
                                             ACT.Exp)
                        act.wait_ge(diff_done, 4 * h + 2 + k + 1)
                        nc.scalar.activation(tmp[:, k, :], tmp[:, k, :], ACT.Exp).then_inc(exp_done, 1)
                    for i in range(2, 4):
                        evacuate(C, i)
                else:
                    for i in range(1, 4):
                        evacuate(C, i)
                    for i in range(2):
                        wait_work(act, h, "keys", i)
                        src = bank("keys", i)[:].rearrange("p (n d) -> p n d", d=DK)
                        for k in range(2):
                            ins = nc.scalar.activation(kw[:, 4 * i:4 * i + 4, k, :], src, ACT.Copy,
                                                       scale=head_cols[:, 2 + k:3 + k])
                        took(ins, "keys", i)
                evacuate(DD, 0)
                split_next(DD)
                evacuate(DD, 1)
                act.wait_ge(squares_done, h + 1)
                nc.scalar.activation(small[:, 1, :], small[:, 0, :], ACT.Sqrt).then_inc(rooted, 1)
                evacuate(DD, 2)
                evacuate(DD, 3)
                for i in range(4):
                    wait_work(act, h, "flip", i)
                    took(nc.scalar.activation(tmp_flat[:, i * 512:i * 512 + 512], bank("flip", i)[:], ACT.Copy,
                                              scale=head_cols[:, i % 2:i % 2 + 1]), "flip", i)
                assert chain.n == n_act

        @block.vector
        def _(dve):
            chain = Chain(dve, dve_chain)

            def split_low(n_total, at):
                dve.wait_ge(w_high, n_total)
                nc.vector.tensor_tensor(w_part[at][1][:], w_raw[:], w_part[at][0][:], ALU.subtract
                                        ).then_inc(w_split, 1)

            if not ret:
                nc.vector.memset(low_rank[0:64, :], 1.0).then_inc(ones_set, 1)
            split_low(1, 0)
            if ret:
                dve.wait_ge(small_in, 64)
                chain.link(nc.vector.tensor_scalar(lt[:, 1], lg[:], 0.0, None, ALU.min))
                dve.wait_ge(act_tables, 1)
                chain.link(nc.vector.tensor_tensor(lt[:, 3], lt[:, 1], lt[:, 0], ALU.subtract))
                for h in range(HEADS):
                    chain.link(nc.vector.tensor_scalar(dists[:, h, :], cst[:, C_AHEAD:C_AHEAD + P],
                                                       lt[:, 3, 0, h:h + 1], None, ALU.mult))
                    ins = nc.vector.scalar_tensor_tensor(out=dists[:, h, :], in0=cst[:, C_BEHIND:C_BEHIND + P],
                                                         scalar=lt[:, 3, 1, h:h + 1], in1=dists[:, h, :],
                                                         op0=ALU.mult, op1=ALU.add)
                ins.then_inc(tables_done, 1)
                ang, turns = curve[:, 1, :], tmp[:, 0, :]
                chain.link(nc.vector.tensor_copy(ang, pos_i[:]))
                chain.link(nc.vector.tensor_scalar(ang, ang, cst[:, C_INV_FREQ:C_INV_FREQ + 1], None, ALU.mult))
                magic = 1.5 * 2.0 ** 23
                chain.link(nc.vector.tensor_scalar(turns, ang, 1.0 / (2 * np.pi), magic, ALU.mult, ALU.add))
                chain.link(nc.vector.tensor_scalar(turns, turns, magic, None, ALU.subtract))
                first = 6.28125
                second = 253.0 * 2.0 ** -17
                third = 2 * np.pi - first - second
                for part in (first, second, third):
                    chain.link(nc.vector.scalar_tensor_tensor(out=ang, in0=turns, scalar=-part, in1=ang,
                                                              op0=ALU.mult, op1=ALU.add))
                cosine, over = curve[:, 0, :], tmp[:, 1, :]
                chain.link(nc.vector.tensor_scalar(cosine, ang, np.pi / 2, None, ALU.add))
                chain.link(nc.vector.tensor_scalar(over, cosine, np.pi, -2 * np.pi, ALU.is_gt, ALU.mult))
                chain.link(nc.vector.tensor_tensor(cosine, cosine, over, ALU.add))
                bound = float(np.nextafter(np.float32(np.pi), np.float32(0)))
                nc.vector.tensor_scalar(curve[:], curve[:], bound, -bound, ALU.min, ALU.max).then_inc(angles_done, 1)
                dve.wait_ge(act_tables, 3)

            chain_base = chain.n
            per = (4 + NT + 1 + 1 + 5 if ret else 4 + NT + 1 + 2 + 5)
            with dve.Fori(0, HEADS) as h:
                chain.start(chain_base + per * h)

                def split_next(tile):
                    split_low(4 * h + tile + 2, (tile + 1) % 2)

                split_next(A)
                if ret:
                    split_next(B)
                    dve.wait_ge(stage_free, h + 1)
                    for i in range(4):
                        w, half = i // 2, slice((i % 2) * 512, (i % 2) * 512 + 512)
                        wait_work(dve, h, "turn", i)
                        took(nc.vector.tensor_tensor(tmp[:, w, half], bank("turn", i)[:], curve[:, 1, half],
                                                     ALU.mult), "turn", i)
                        dst = (qd, kd)[w][:, 0, half]
                        chain.link(nc.vector.tensor_tensor(dst, qk_raw[:, w, half], curve[:, 0, half], ALU.mult))
                        nc.vector.tensor_tensor(dst, dst, tmp[:, w, half], ALU.add).then_inc(roped, 1)
                    split_next(C)
                    dve.wait_ge(roped, 4 * h + 4)
                    for k in range(2):
                        ins = nc.vector.tensor_tensor(
                            qw[:, k, :].rearrange("p (n i) -> p n i", i=P),
                            qd[:, 0, :].rearrange("p (n i) -> p n i", i=P),
                            rows[:, bass.ds(h, 1), k, :].to_broadcast([P, NT, P]), ALU.mult)
                    ins.then_inc(q_weighted, 1)
                else:
                    for i in range(4):
                        dve.wait_ge(z_folded, 4 * h + i + 1)
                        took(nc.vector.tensor_scalar(kw_flat[:, i * 512:i * 512 + 512], bank("gate", i)[:], 0.0,
                                                     1.0 / GATE_NORMALIZER, ALU.min, ALU.mult), "gate", i)
                    wait_taken(dve, h, "gate", 3)
                    wait_taken(dve, h, "gate", 2)
                    dve.wait_ge(act_chain, 2 * h + 2)
                    nc.vector.scalar_tensor_tensor(out=tmp_flat, in0=tmp_flat, scalar=-1.0 / GATE_NORMALIZER,
                                                   in1=kw_flat, op0=ALU.mult, op1=ALU.add).then_inc(decay_logs, 1)
                    split_next(B)

                    def cum(k):
                        return curve[:, k, :].rearrange("p (n i) -> p n i", i=P)

                    def diff(k):
                        return tmp[:, k, :].rearrange("p (n i) -> p n i", i=P)

                    for k in range(2):
                        wait_taken(dve, h, "cum", 2 * k)
                        wait_taken(dve, h, "cum", 2 * k + 1)
                        if k == 0:
                            wait_work(dve, h, "cum", 3)
                        mid = P // 2 if k == 0 else P // 2 - 1
                        nc.vector.tensor_tensor(diff(k), cum(k), cum(k)[:, :, mid:mid + 1].to_broadcast([P, NT, P]),
                                                ALU.subtract).then_inc(diff_done, 1)
                    split_next(C)
                    for k in range(2):
                        dve.wait_ge(exp_done, 4 * h + k + 1)
                        last = P - 1 if k == 0 else 0
                        nc.vector.tensor_tensor(diff(k), cum(k)[:, :, last:last + 1].to_broadcast([P, NT, P]), cum(k),
                                                ALU.subtract).then_inc(diff_done, 1)
                        nc.vector.tensor_tensor(qd[:, k, :], qd[:, k, :], qk_raw[:, 0, :], ALU.mult)
                        nc.vector.tensor_tensor(kd[:, k, :], kd[:, k, :], qk_raw[:, 1, :], ALU.mult)
                    for k in range(2):
                        dve.wait_ge(exp_done, 4 * h + 2 + k + 1)
                        nc.vector.tensor_tensor(tmp[:, k, :], tmp[:, k, :], qk_raw[:, 1, :], ALU.mult)
                        ins = nc.vector.tensor_tensor(qw[:, k, :], qw[:, k, :], qk_raw[:, 0, :], ALU.mult)
                        ins.then_inc(keys_weighted, 1)
                    for i in range(4):
                        wait_work(dve, h, "keys", i)
                        took(nc.vector.tensor_copy(kw_flat[:, i * 512:i * 512 + 512], bank("keys", i)[:]), "keys", i)
                for i in range(NT - 1):
                    wait_work(dve, h, "state", i)
                    src = bank("state", i)
                    back = NT - 2 - i
                    if i == 0:
                        nc.vector.tensor_copy(states[:, 0, 0, :], src[:, 0:DV]).then_inc(state_f, 1)
                        took(nc.vector.tensor_copy(states[:, 1, back, :], src[:, DV:2 * DV]), "state", i)
                        continue
                    wait_taken(dve, h, "state", i - 1)
                    d_f = dec[:, 0, bass.ds(h, 1)] if ret else dec[:, 0, i:i + 1]
                    d_b = dec[:, 1, bass.ds(h, 1)] if ret else dec[:, 1, back + 1:back + 2]
                    nc.vector.scalar_tensor_tensor(out=states[:, 0, i, :], in0=states[:, 0, i - 1, :], scalar=d_f,
                                                   in1=src[:, 0:DV], op0=ALU.mult, op1=ALU.add).then_inc(state_f, 1)
                    took(nc.vector.scalar_tensor_tensor(out=states[:, 1, back, :], in0=states[:, 1, back + 1, :],
                                                        scalar=d_b, in1=src[:, DV:2 * DV], op0=ALU.mult,
                                                        op1=ALU.add), "state", i)
                split_next(DD)
                if ret:
                    for i in range(2):
                        wait_work(dve, h, "score", i)
                        took(nc.vector.tensor_tensor(probs[:, 4 * i:4 * i + 4, :],
                                                     bank("score", i)[:].rearrange("p (n i) -> p n i", i=P),
                                                     dists[:, bass.ds(h, 1), :].to_broadcast([P, 4, P]), ALU.mult),
                             "score", i)
                else:
                    for i in range(4):
                        wait_work(dve, h, "score", i)
                        nc.vector.memset(small[:, 3, i:i + 1], 0.0)
                        src = bank("score", i)[:].rearrange("p (n w i) -> p n w i", n=2, w=2)
                        for k, c in enumerate((C_UPTO, C_AFTER)):
                            mask = cst[:, c:c + P].bitcast(U32).unsqueeze(1).to_broadcast([P, 2, P])
                            ins = nc.vector.copy_predicated(probs[:, 2 * i:2 * i + 2, :], mask, src[:, :, k, :])
                            if k == 0:
                                chain.link(ins)
                                nc.vector.memset(small[:, 3, 4 + i:5 + i], 0.0)
                        took(ins, "score", i)
                for n in range(NT):
                    if n % 2 == 0:
                        dve.wait_ge(out_done, NT * h + n + 2)
                    chain.wait()
                    chain.mark(nc.vector.bn_stats(stats[:, n, :], out[:, n, :]))
                    if n:
                        nc.vector.bn_aggr(mv[:, n - 1, :], stats[:, n - 1, :])
                chain.wait()
                nc.vector.memset(small[:, 3, :], 0.0)
                chain.link(nc.vector.bn_aggr(mv[:, NT - 1, :], stats[:, NT - 1, :]))
                if ret:
                    chain.mark(nc.vector.tensor_scalar(small[:, 0, :], mv[:, :, 1], EPS, None, ALU.add))
                    chain.wait()
                    nc.vector.tensor_copy(small[:, 3, :], mv[:, :, 0]).then_inc(squares_done, 1)
                else:
                    chain.link(nc.vector.tensor_tensor(small[:, 0, :], mv[:, :, 0], mv[:, :, 0], ALU.mult))
                    chain.link(nc.vector.tensor_tensor(small[:, 0, :], small[:, 0, :], mv[:, :, 1], ALU.add))
                    nc.vector.tensor_scalar(small[:, 0, :], small[:, 0, :], EPS, None, ALU.add
                                            ).then_inc(squares_done, 1)
                dve.wait_ge(rooted, h + 1)
                inverse_root(nc, chain, small[:, 2, :], small[:, 1, :], small[:, 0, :], small[:, 1, :])
                for n in range(NT):
                    if ret:
                        ins = nc.vector.tensor_scalar(o_n[:, n, :], out[:, n, :], small[:, 3, n:n + 1],
                                                      small[:, 2, n:n + 1], ALU.subtract, ALU.mult)
                    else:
                        ins = nc.vector.tensor_scalar(o_n[:, n, :], out[:, n, :], small[:, 2, n:n + 1], None, ALU.mult)
                    if n % 4 == 3:
                        ins.then_inc(out_normed, 1)
                for half in range(2):
                    dve.wait_ge(out_normed, 2 * h + half + 1)
                    at = slice(4 * half, 4 * half + 4)
                    nc.vector.tensor_tensor(o_n[:, at, :], o_n[:, at, :], g_sb[:, at, :], ALU.mult
                                            ).then_inc(out_gated, 1)
                assert chain.n == per, (chain.n, per)

        @block.tensor
        def _(pe):
            ps = lambda h_, u: pe.wait_ge(proj_taken, 16 * h_ + u + 1)
            if not ret:
                pe.wait_ge(small_in, 96)
                for u in range(4):
                    k, half = u // 2, u % 2
                    if u >= 2:
                        pe.wait_ge(low_taken, u - 1)
                    for kc in range(KC):
                        for part in range(2):
                            last = nc.tensor.matmul(proj[u % 2][32 * k:32 * k + RANK, :],
                                                    wa_raw[:, kc, RANK * k:RANK * k + RANK],
                                                    hT[part][:, kc, half * 512:half * 512 + 512].bitcast(F32),
                                                    start=kc == 0 and part == 0, stop=kc == KC - 1 and part == 1)
                    last.then_inc(low_done, 1)
                pe.wait_ge(low_taken, 4)

            with pe.Fori(0, HEADS) as h:
                def project(tile, i):
                    if i == 0:
                        pe.wait_ge(w_split, 4 * h + tile + 1)
                    pe.wait_ge(proj_taken, 16 * h + proj_unit(tile, i) + 1)
                    w = w_part[tile % 2]
                    if tile == A:
                        c0 = DK * (i // 2)
                        last = product(nc, proj[i % 2][:], w, hT, lambda x, kc: x[:, kc, c0:c0 + DK],
                                       lambda y, kc: y[:, kc, (i % 2) * 512:(i % 2) * 512 + 512])
                    else:
                        for t in range(2 * i, 2 * i + 2):
                            last = product(nc, proj[i % 2][:, (t % 2) * COLS:(t % 2) * COLS + COLS], hT, w,
                                           lambda x, kc: x[:, kc, t * P:(t + 1) * P], lambda y, kc: y[:, kc, :])
                    last.then_inc(proj_done, 1)

                def begin(kind, i):
                    n = order[(kind, i)]
                    pe.wait_ge(work_taken[n % 2], uses[n % 2] * h + n // 2 + 1)
                    return bank(kind, i)

                for i in range(4):
                    project(A, i)
                if not ret:
                    pe.wait_ge(gate_ready, h + 1)
                    for i in range(4):
                        dst = begin("gate", i)
                        k = i % 2
                        for n in range(4):
                            t = 4 * (i // 2) + n
                            last = nc.tensor.matmul(dst[:, n * DK:(n + 1) * DK],
                                                    low_rank[32 * k:32 * k + RANK + 1, t * P:(t + 1) * P],
                                                    gate_head[32 * k:32 * k + RANK + 1, :], start=True, stop=True)
                        last.then_inc(work_done, 1)
                for i in range(4):
                    project(B, i)
                if ret:
                    for i in range(4):
                        dst = begin("turn", i)
                        pe.wait_ge(proj_taken, 16 * h + i + 1 + 2)
                        nc.tensor.matmul(dst[:], cst[:, C_ROT:C_ROT + P],
                                         qk_raw[:, i // 2, (i % 2) * 512:(i % 2) * 512 + 512],
                                         start=True, stop=True).then_inc(work_done, 1)
                else:
                    pe.wait_ge(decay_logs, h + 1)
                    for i in range(4):
                        dst = begin("cum", i)
                        k = i // 2
                        tri = cst[:, (C_UPTO, C_FROM)[k]:(C_UPTO, C_FROM)[k] + P]
                        for n in range(4):
                            c = 4 * (i % 2) + n
                            at = 512 * (2 * (c // 4) + k) + DK * (c % 4)
                            last = nc.tensor.matmul(dst[:, n * P:(n + 1) * P], tmp_flat[:, at:at + DK], tri,
                                                    start=True, stop=True)
                        last.then_inc(work_done, 1)
                for i in range(4):
                    project(C, i)
                if ret:
                    for i in range(2):
                        dst = begin("keys", i)
                        pe.wait_ge(roped, 4 * h + 2 + i + 1)
                        for n in range(4):
                            c = 4 * i + n
                            last = nc.tensor.transpose(dst[:, n * P:(n + 1) * P], kd[:, 0, c * P:(c + 1) * P], ident)
                        last.then_inc(work_done, 1)
                    for i in range(2):
                        project(DD, i)
                else:
                    for i in range(2):
                        project(DD, i)
                    pe.wait_ge(keys_weighted, 2 * h + 2)
                    for i in range(4):
                        dst = begin("keys", i)
                        for n in range(2):
                            for k in range(2):
                                c = 2 * i + n
                                last = nc.tensor.transpose(dst[:, (2 * n + k) * DK:(2 * n + k + 1) * DK],
                                                           tmp[:, k, c * P:(c + 1) * P], ident)
                        last.then_inc(work_done, 1)
                for i in range(NT - 1):
                    dst = begin("state", i)
                    if i == 0:
                        pe.wait_ge(proj_taken, 16 * h + proj_unit(B, 3) + 1 + 2)
                        for j in range(2 if ret else 4):
                            wait_taken(pe, h, "keys", j)
                    for k, c in ((0, i), (1, NT - 1 - i)):
                        last = nc.tensor.matmul(dst[:, k * DV:(k + 1) * DV], kw[:, c, k, :], v_sb[:, c, :],
                                                start=True, stop=True)
                    last.then_inc(work_done, 1)
                if ret:
                    for i in range(2):
                        dst = begin("score", i)
                        for n in range(4):
                            c = slice((4 * i + n) * P, (4 * i + n + 1) * P)
                            last = nc.tensor.matmul(dst[:, n * P:(n + 1) * P], kd[:, 0, c], qd[:, 0, c],
                                                    start=True, stop=True)
                        last.then_inc(work_done, 1)
                    pe.wait_ge(q_weighted, h + 1)
                else:
                    for i in range(4):
                        dst = begin("score", i)
                        for n in range(2):
                            for k in range(2):
                                c = slice((2 * i + n) * P, (2 * i + n + 1) * P)
                                last = nc.tensor.matmul(dst[:, (2 * n + k) * P:(2 * n + k + 1) * P], kd[:, k, c],
                                                        qd[:, k, c], start=True, stop=True)
                        last.then_inc(work_done, 1)
                wait_taken(pe, h, "state", NT - 2)
                for n in range(NT):
                    per_unit = 4 if ret else 2
                    if n % per_unit == 0:
                        wait_taken(pe, h, "score", n // per_unit)
                    c = slice(n * P, (n + 1) * P)
                    terms = [(probs[:, n, :], v_sb[:, n, :])]
                    if n > 0:
                        terms.append((qw[:, 0, c], states[:, 0, n - 1, :]))
                    if n < NT - 1:
                        terms.append((qw[:, 1, c], states[:, 1, n, :]))
                    for j, (x, y) in enumerate(terms):
                        last = nc.tensor.matmul(out[:, n, :], x, y, start=j == 0, stop=j == len(terms) - 1)
                    last.then_inc(out_done, 1)
                for i in range(2, 4):
                    project(DD, i)
                for i in range(4):
                    dst = begin("flip", i)
                    half, e = i // 2, i % 2
                    pe.wait_ge(out_gated, 2 * h + half + 1)
                    for n in range(4):
                        last = nc.tensor.transpose(dst[:, n * P:(n + 1) * P],
                                                   o_n[:, 4 * half + n, e * P:(e + 1) * P], ident)
                    last.then_inc(work_done, 1)


def merge_and_route(nc, sems, x, ret_T, gla_T, gates, w_branches, w_out, norm_ffn, w_router, cst, affinity, x_mid, h_mid):
    PAIRS = D // COLS // 2
    with ExitStack() as ctx:
        sb = lambda n, s, d=F32: ctx.enter_context(nc.sbuf_tensor(f"m_{n}", s, d))
        sem = lambda n: sems.enter_context(nc.semaphore(f"m_{n}"))
        psum = lambda n, s: ctx.enter_context(nc.psum_tensor(f"m_{n}", s, F32))
        w_raw = sb("w_raw", [P, KC, COLS])
        w_part = [[sb(f"w_part{i}{k}", [P, KC, COLS], F32R) for k in range(2)] for i in range(2)]
        x_raw = sb("x_raw", [P, 2, SEQ])
        xT = [sb(f"xT{k}", [P, KC, SEQ], F32R) for k in range(2)]
        merged = sb("merged", [P, NT, D])
        side = sb("side", [P, 4, 2, COLS])
        prod = sb("prod", [P, 2, 2, COLS])
        h2 = sb("h2", [P, 2, D])
        h2T = sb("h2T", [P, 2, KC, P])
        gain_row = sb("gain_row", [P, D])
        router = sb("router", [P, KC, EXPERTS])
        stat = sb("stat", [P, 5, NT])
        logit = sb("logit", [P, NT, EXPERTS])
        peak = sb("peak", [P, 3, NT])
        proj = [psum(f"proj{b}", [P, 512]) for b in range(2)]
        work = [psum(f"work{b}", [P, 4, P]) for b in range(2)]
        logits = psum("logits", [P, NT, EXPERTS])
        turned = [psum(f"turned{b}", [EXPERTS, 4, P]) for b in range(2)]

        w_loaded = sem("w_loaded")
        w_high = sem("w_high")
        w_split = sem("w_split")
        x_loaded = [sem(f"x_loaded{i}") for i in range(2)]
        x_high = sem("x_high")
        x_split = sem("x_split")
        side_in = [sem(f"side_in{i}") for i in range(4)]
        proj_done = sem("proj_done")
        proj_taken = sem("proj_taken")
        summed = sem("summed")
        x_mid_done = sem("x_mid_done")
        merged_T = sem("merged_T")
        m_high = sem("m_high")
        m_low = sem("m_low")
        small_in = sem("small_in")
        squared = sem("squared")
        meaned = sem("meaned")
        rooted = sem("rooted")
        normed = sem("normed")
        h_turned = sem("h_turned")
        h_copied = sem("h_copied")
        logits_done = sem("logits_done")
        x_stored = sem("x_stored")
        h_stored = sem("h_stored")
        shifted = sem("shifted")
        exped = sem("exped")
        softmaxed = sem("softmaxed")
        aff_turned = sem("aff_turned")
        aff_done = sem("aff_done")
        dve_chain = sem("dve_chain")
        ident = cst[:, C_IDENT:C_IDENT + P]
        block = ctx.enter_context(nc.Block())
        tiles = [(phase, g, j) for phase in range(3) for g in range(PAIRS) for j in range(2)]

        @block.sync
        def _(sp):
            def load_w(w, c):
                sp.dma_start(w_raw[:], w[0].rearrange("(c p) n -> p c n", p=P)[:, :, bass.ds(c * COLS, COLS)]
                             ).then_inc(w_loaded, 16)

            def load_x(n, src):
                sp.dma_start(x_raw[:, n % 2], src[n % KC]).then_inc(x_loaded[n % 2], 16)

            for phase, w in enumerate((*w_branches, w_out)):
                if phase:
                    sp.wait_ge(w_split, 4 * phase)
                load_w(w, 0)
                if phase < 2:
                    src = (ret_T, gla_T)[phase]
                    for kc in range(KC):
                        n = KC * phase + kc
                        if n >= 2:
                            sp.wait_ge(x_split, n - 1)
                        load_x(n, src)
                if phase == 0:
                    sp.dma_start(gain_row[:], norm_ffn.to_broadcast([P, D])).then_inc(small_in, 16)
                    sp.dma_start(router[:], w_router[0].rearrange("(c p) n -> p c n", p=P)).then_inc(small_in, 16)
                for c in range(1, 4):
                    sp.wait_ge(w_split, 4 * phase + c)
                    load_w(w, c)
            sp.wait_ge(w_split, 12)
            load_w(w_out, 0)

        @block.scalar
        def _(act):
            act.sem_inc(proj_taken, 4)

            def split_w(n, at):
                act.wait_ge(w_loaded, 16 * (n + 1))
                nc.scalar.activation(w_part[at][0][:], w_raw[:], ACT.Copy).then_inc(w_high, 1)

            def load_side(n, phase, c):
                for i in range(4):
                    act.wait_ge(proj_taken, 4 * n + i + 1)
                    src = (gates if phase < 2 else x[0]).rearrange("(t p) n -> p t n", p=P)
                    act.dma_start(side[:, i], src[:, 2 * i:2 * i + 2,
                                                  bass.ds(c * COLS + (D if phase == 1 else 0), COLS)]
                                  ).then_inc(side_in[i], 16)

            split_w(0, 0)
            for phase in range(3):
                if phase < 2:
                    for kc in range(KC):
                        n = KC * phase + kc
                        act.wait_ge(x_loaded[n % 2], 16 * (n // 2 + 1))
                        if phase == 1 and kc == 0:
                            act.wait_ge(proj_done, 16)
                        nc.scalar.activation(xT[0][:, kc, :], x_raw[:, n % 2], ACT.Copy).then_inc(x_high, 1)
                else:
                    for u in range(2 * NT):
                        act.wait_ge(merged_T, u + 1)
                        t, c0 = u // 2, 4 * (u % 2)
                        nc.scalar.activation(xT[0][:, c0:c0 + 4, t * P:(t + 1) * P], work[u % 2][:], ACT.Copy
                                             ).then_inc(m_high, 1)
                with act.Fori(0, PAIRS) as g:
                    for j in range(2):
                        n = 2 * g + (4 * phase + j)
                        load_side(n, phase, 2 * g + j)
                        act.wait_ge(proj_done, 4 * n + 1)
                        split_w(n + 1, (j + 1) % 2)
            for t in range(NT):
                act.wait_ge(x_mid_done, 1)
                if t >= 2:
                    act.wait_ge(h_stored, 16 * (t - 1))
                    act.wait_ge(h_turned, 2 * (t - 1))
                nc.scalar.activation(h2[:, t % 2], merged[:, t, :], ACT.Square,
                                     accum_out=stat[:, 0, t:t + 1]).then_inc(squared, 1)
                act.wait_ge(meaned, t + 1)
                nc.scalar.activation(stat[:, 1, t:t + 1], stat[:, 3, t:t + 1], ACT.Sqrt).then_inc(rooted, 1)
                for half in range(2):
                    u = 2 * t + half
                    act.wait_ge(h_turned, u + 1)
                    nc.scalar.activation(h2T[:, t % 2, 4 * half:4 * half + 4, :], work[u % 2][:], ACT.Copy
                                         ).then_inc(h_copied, 1)
            act.wait_ge(shifted, 1)
            nc.scalar.activation(logit[:], logit[:], ACT.Exp).then_inc(exped, 1)
            for b in range(2):
                act.wait_ge(aff_turned, b + 1)
                nc.scalar.activation(affinity[:, 512 * b:512 * b + 512].rearrange("e (t p) -> e t p", p=P),
                                     turned[b][:], ACT.Copy).then_inc(aff_done, 1)

        @block.gpsimd
        def _(pool):
            for t in range(NT):
                if t == 0:
                    pool.wait_ge(x_mid_done, 1)
                pool.dma_start(x_mid[t * P:(t + 1) * P, :], merged[:, t, :]).then_inc(x_stored, 16)
                pool.wait_ge(normed, t + 1)
                pool.dma_start(h_mid[t * P:(t + 1) * P, :], h2[:, t % 2]).then_inc(h_stored, 16)
                pool.wait_ge(h_stored, 16 * (t + 1))
            pool.wait_ge(x_stored, 16 * NT)

        @block.vector
        def _(dve):
            chain = Chain(dve, dve_chain)

            def split_w(n, at):
                dve.wait_ge(w_high, n + 1)
                nc.vector.tensor_tensor(w_part[at][1][:], w_raw[:], w_part[at][0][:], ALU.subtract
                                        ).then_inc(w_split, 1)

            split_w(0, 0)
            for phase in range(3):
                if phase < 2:
                    for kc in range(KC):
                        n = KC * phase + kc
                        dve.wait_ge(x_high, n + 1)
                        nc.vector.tensor_tensor(xT[1][:, kc, :], x_raw[:, n % 2], xT[0][:, kc, :], ALU.subtract
                                                ).then_inc(x_split, 1)
                else:
                    for u in range(2 * NT):
                        dve.wait_ge(m_high, u + 1)
                        at = (slice(None), slice(4 * (u % 2), 4 * (u % 2) + 4), slice(u // 2 * P, (u // 2 + 1) * P))
                        nc.vector.tensor_tensor(xT[1][at], work[u % 2][:], xT[0][at], ALU.subtract
                                                ).then_inc(m_low, 1)
                with dve.Fori(0, PAIRS) as g:
                    for j in range(2):
                        n = 2 * g + (4 * phase + j)
                        for i in range(4):
                            dve.wait_ge(proj_done, 4 * n + i + 1)
                            dve.wait_ge(side_in[i], 16 * n + 16)
                            dst = merged[:, 2 * i:2 * i + 2, bass.ds((2 * g + j) * COLS, COLS)]
                            src = proj[i % 2][:].rearrange("p (t n) -> p t n", t=2)
                            if phase == 0:
                                nc.vector.tensor_tensor(dst, src, side[:, i], ALU.mult).then_inc(proj_taken, 1)
                            elif phase == 1:
                                nc.vector.tensor_tensor(prod[:, i % 2], src, side[:, i], ALU.mult
                                                        ).then_inc(proj_taken, 1)
                                dve.wait_ge(proj_taken, 4 + 4 * n + i + 1)
                                nc.vector.tensor_tensor(dst, dst, prod[:, i % 2], ALU.add).then_inc(summed, 1)
                            else:
                                nc.vector.tensor_tensor(dst, src, side[:, i], ALU.add).then_inc(proj_taken, 1)
                            if i == 0:
                                split_w(n + 1, (j + 1) % 2)
            chain.link(nc.vector.memset(peak[:], 0.0))
            dve.wait_ge(proj_taken, 4 + 48)
            dve.sem_inc(x_mid_done, 1)
            dve.wait_ge(small_in, 32)
            for t in range(NT):
                dve.wait_ge(squared, t + 1)
                nc.vector.tensor_scalar(stat[:, 3, t:t + 1], stat[:, 0, t:t + 1], 1.0 / D, EPS,
                                        ALU.mult, ALU.add).then_inc(meaned, 1)
                dve.wait_ge(rooted, t + 1)
                inverse_root(nc, chain, stat[:, 2, t:t + 1], stat[:, 1, t:t + 1],
                             stat[:, 3, t:t + 1], stat[:, 4, t:t + 1])
                nc.vector.scalar_tensor_tensor(out=h2[:, t % 2], in0=merged[:, t, :], scalar=stat[:, 2, t:t + 1],
                                               in1=gain_row[:], op0=ALU.mult, op1=ALU.mult).then_inc(normed, 1)
            dve.wait_ge(logits_done, NT)
            wide = lambda a: a.unsqueeze(2).to_broadcast([P, NT, EXPERTS])
            chain.link(nc.vector.tensor_reduce(peak[:, 0, :], logits[:], AX_X, ALU.max))
            nc.vector.tensor_tensor(logit[:], logits[:], wide(peak[:, 0, :]), ALU.subtract).then_inc(shifted, 1)
            dve.wait_ge(exped, 1)
            chain.link(nc.vector.tensor_reduce(peak[:, 1, :], logit[:], AX_X, ALU.add))
            chain.link(nc.vector.reciprocal(peak[:, 2, :], peak[:, 1, :]))
            nc.vector.tensor_tensor(logit[:], logit[:], wide(peak[:, 2, :]), ALU.mult).then_inc(softmaxed, 1)

        @block.tensor
        def _(pe):
            for phase in range(3):
                if phase == 2:
                    pe.wait_ge(summed, 16)
                    for u in range(2 * NT):
                        if u >= 2:
                            pe.wait_ge(m_low, u - 1)
                        for c in range(4):
                            kc = 4 * (u % 2) + c
                            last = nc.tensor.transpose(work[u % 2][:, c, :],
                                                       merged[:, u // 2, kc * P:(kc + 1) * P], ident)
                        last.then_inc(merged_T, 1)
                    pe.wait_ge(m_low, 2 * NT)
                else:
                    pe.wait_ge(x_split, KC * (phase + 1))
                with pe.Fori(0, PAIRS) as g:
                    for j in range(2):
                        n = 2 * g + (4 * phase + j)
                        pe.wait_ge(w_split, n + 1)
                        for i in range(4):
                            pe.wait_ge(proj_taken, 4 * n + i + 3)
                            for t in range(2 * i, 2 * i + 2):
                                last = product(nc, proj[i % 2][:, (t % 2) * COLS:(t % 2) * COLS + COLS], xT, w_part[j],
                                               lambda a, kc: a[:, kc, t * P:(t + 1) * P], lambda a, kc: a[:, kc, :])
                            last.then_inc(proj_done, 1)
            pe.wait_ge(small_in, 32)
            for t in range(NT + 1):
                if t < NT:
                    pe.wait_ge(normed, t + 1)
                    for half in range(2):
                        u = 2 * t + half
                        if u >= 2:
                            pe.wait_ge(h_copied, u - 1)
                        for c in range(4):
                            kc = 4 * half + c
                            last = nc.tensor.transpose(work[u % 2][:, c, :], h2[:, t % 2, kc * P:(kc + 1) * P], ident)
                        last.then_inc(h_turned, 1)
                if t:
                    pe.wait_ge(h_copied, 2 * t)
                    for kc in range(KC):
                        last = nc.tensor.matmul(logits[:, t - 1, :], h2T[:, (t - 1) % 2, kc, :], router[:, kc, :],
                                                start=kc == 0, stop=kc == KC - 1)
                    last.then_inc(logits_done, 1)
            pe.wait_ge(softmaxed, 1)
            for b in range(2):
                for c in range(4):
                    last = nc.tensor.transpose(turned[b][:, c, :], logit[:, 4 * b + c, :], ident)
                last.then_inc(aff_turned, 1)


def experts(nc, sems, affinity, cst, x_mid, h_mid, w_gate, w_up, w_down):
    FT = COLS
    TILES = D_FF // FT
    UNITS = 3 * TILES
    RAW, PARTS, AHEAD = 11, 3, 2
    assert UNITS % RAW == 0 and UNITS % PARTS == 0 and D_FF % FT == 0
    order = [("gate", 0), ("up", 0)]
    for i in range(1, TILES):
        order += [("gate", i), ("up", i), ("down", i - 1)]
    order.append(("down", TILES - 1))
    place = {u: k for k, u in enumerate(order)}
    ROUNDS = CAPACITY // 8

    with ExitStack() as ctx:
        sb = lambda n, s, d=F32: ctx.enter_context(nc.sbuf_tensor(f"e_{n}", s, d))
        sem = lambda n: sems.enter_context(nc.semaphore(f"e_{n}"))
        psum = lambda n, s: ctx.enter_context(nc.psum_tensor(f"e_{n}", s, F32))
        raw = [sb(f"raw{s}", [P, KC * FT]) for s in range(RAW)]
        part = [[sb(f"part{s}{k}", [P, KC * FT], F32R) for k in range(2)] for s in range(PARTS)]
        xg = sb("xg", [P, D])
        xgT = [sb(f"xgT{k}", [P, KC, P], F32R) for k in range(2)]
        silu = sb("silu", [P, 2, FT])
        act_sb = sb("act", [P, 2, FT])
        actT = [sb(f"actT{k}", [P, 2, P], F32R) for k in range(2)]
        y_sb = sb("y", [P, D])
        left = [sb(f"left{k}", [EXPERTS, SEQ]) for k in range(2)]
        top = sb("top", [EXPERTS, CAPACITY])
        top_at = sb("top_at", [EXPERTS, CAPACITY], U32)
        top_at_f = sb("top_at_f", [EXPERTS, CAPACITY])
        weight = sb("weight", [P, EXPERTS])
        token = sb("token", [P, EXPERTS], U32)
        weight_now = sb("weight_now", [P, 1])
        token_now = sb("token_now", [P, 1], U32)
        token_next = sb("token_next", [P, 1], U32)
        idle = sb("idle", [P, 2])
        pool_idle = sb("pool_idle", [P, 2])
        pre = [psum(f"pre{b}", [P, 2, FT]) for b in range(2)]
        turn = psum("turn", [P, 2, P])
        x_turn = [psum(f"x_turn{b}", [P, 4, P]) for b in range(2)]
        y_ps = psum("y_ps", [P, 2, 512])

        raw_in = [sem(f"raw_in{s}") for s in range(RAW)]
        w_high = sem("w_high")
        w_split = sem("w_split")
        unit_done = sem("unit_done")
        silu_done = sem("silu_done")
        act_done = sem("act_done")
        act_turned = sem("act_turned")
        act_high = sem("act_high")
        act_split = sem("act_split")
        gathered = sem("gathered")
        x_turned = sem("x_turned")
        x_high = sem("x_high")
        x_split = sem("x_split")
        y_taken = sem("y_taken")
        scattered = sem("scattered")
        y_free = sem("y_free")
        chosen = sem("chosen")
        lists_turned = sem("lists_turned")
        indices_next = sem("indices_next")
        indices_now = sem("indices_now")
        dve_chain = sem("dve_chain")
        carried = sem("carried")
        ident = cst[:, C_IDENT:C_IDENT + P]
        block = ctx.enter_context(nc.Block())

        def loop(eng, body):
            with eng.Fori(0, EXPERTS - 1) as e:
                body(e, False)
            body(EXPERTS - 1, True)

        @block.sync
        def _(sp):
            def load(e, k):
                kind, i = order[k]
                if kind == "down":
                    src = w_down[0][bass.ds(e, 1), i * FT:(i + 1) * FT, :].rearrange("e (j p) n -> p (e j) n", p=P)
                    dst = raw[k % RAW][:].rearrange("p (j n) -> p j n", j=2)
                else:
                    w = w_gate if kind == "gate" else w_up
                    src = w[0][bass.ds(e, 1), :, i * FT:(i + 1) * FT].rearrange("e (c p) n -> p (e c) n", p=P)
                    dst = raw[k % RAW][:].rearrange("p (c n) -> p c n", c=KC)
                sp.dma_start(dst, src).then_inc(raw_in[k % RAW], 16)

            for k in range(RAW):
                load(0, k)

            def body(e, last):
                for k in range(UNITS - RAW if last else UNITS):
                    sp.wait_ge(w_split, UNITS * e + k + 1)
                    load(e + (k + RAW) // UNITS, (k + RAW) % UNITS)

            loop(sp, body)

        @block.gpsimd
        def _(pool):
            pool.sem_inc(y_free, 1)

            def carry_wait(at):
                nc.gpsimd.tensor_tensor(pool_idle[:, at:at + 1], cst[:, C_EPS:C_EPS + 1], cst[:, C_EPS:C_EPS + 1],
                                        ALU.add).then_inc(carried, 1)

            def gather():
                pool.indirect_dma_start(xg[:], None, h_mid, bass.IndirectOffsetOnAxis(ap=token_next[:, 0:1], axis=0)
                                        ).then_inc(gathered, 16)

            pool.wait_ge(indices_next, 1)
            gather()

            def body(e, last):
                if not last:
                    pool.wait_ge(indices_next, e + 2)
                    pool.wait_ge(x_turned, 2 * e + 2)
                    carry_wait(0)
                    gather()
                pool.wait_ge(indices_now, e + 1)
                pool.wait_ge(y_taken, e + 2)
                pool.wait_ge(carried, 2 * e + (0 if last else 1))
                carry_wait(1)
                pool.indirect_dma_start(x_mid, bass.IndirectOffsetOnAxis(ap=token_now[:, 0:1], axis=0), y_sb[:], None,
                                        compute_op=ALU.add).then_inc(scattered, 16)
                pool.wait_ge(scattered, 16 * e + 16)
                pool.sem_inc(y_free, 1)

            loop(pool, body)

        @block.scalar
        def _(act):
            act.sem_inc(y_taken, 1)

            def split_high(e, k):
                n = UNITS * e + k
                act.wait_ge(raw_in[k % RAW], 16 * (UNITS // RAW) * e + 16 * (k // RAW + 1))
                act.wait_ge(unit_done, n + 1)
                nc.scalar.activation(part[k % PARTS][0][:], raw[k % RAW][:], ACT.Copy).then_inc(w_high, 1)

            def x_part(e, u):
                act.wait_ge(x_turned, 2 * e + u + 1)
                nc.scalar.activation(xgT[0][:, 4 * u:4 * u + 4, :], x_turn[u][:], ACT.Copy).then_inc(x_high, 1)

            for k in range(AHEAD):
                split_high(0, k)
            for u in range(2):
                x_part(0, u)

            def body(e, last):
                for p in range(UNITS):
                    k = p + AHEAD
                    if k < UNITS:
                        split_high(e, k)
                    elif not last:
                        split_high(e + 1, k - UNITS)
                    for i in range(TILES):
                        if p == place["up", i] + 1:
                            act.wait_ge(unit_done, PARTS + UNITS * e + p)
                            nc.scalar.activation(silu[:, i % 2], pre[i % 2][:, 0, :], ACT.Silu).then_inc(silu_done, 1)
                        if p == (place["up", i + 1] if i < TILES - 1 else place["down", i]):
                            act.wait_ge(act_turned, TILES * e + i + 1)
                            nc.scalar.activation(actT[0][:], turn[:], ACT.Copy).then_inc(act_high, 1)
                if not last:
                    for u in range(2):
                        x_part(e + 1, u)
                act.wait_ge(unit_done, PARTS + UNITS * e + UNITS)
                act.wait_ge(y_free, e + 1)
                act.wait_ge(indices_now, e + 1)
                for half in range(2):
                    ins = nc.scalar.activation(y_sb[:, 512 * half:512 * half + 512], y_ps[:, half, :], ACT.Copy,
                                               scale=weight_now[:, 0:1])
                ins.then_inc(y_taken, 1)

            loop(act, body)

        @block.vector
        def _(dve):
            chain = Chain(dve, dve_chain)
            dve.sem_inc(act_done, 2)
            dve.sem_inc(act_split, 1)

            def split_low(e, k):
                dve.wait_ge(w_high, UNITS * e + k + 1)
                nc.vector.tensor_tensor(part[k % PARTS][1][:], raw[k % RAW][:], part[k % PARTS][0][:], ALU.subtract
                                        ).then_inc(w_split, 1)

            def x_part(e, u):
                dve.wait_ge(x_high, 2 * e + u + 1)
                nc.vector.tensor_tensor(xgT[1][:, 4 * u:4 * u + 4, :], x_turn[u][:], xgT[0][:, 4 * u:4 * u + 4, :],
                                        ALU.subtract).then_inc(x_split, 1)

            for k in range(AHEAD):
                split_low(0, k)
            now = affinity
            for r in range(ROUNDS):
                eight = slice(8 * r, 8 * r + 8)
                chain.link(nc.vector.max(top[:, eight], now[:]))
                chain.mark(nc.vector.max_index(top_at[:, eight], top[:, eight], now[:]))
                if r < ROUNDS - 1:
                    chain.link(nc.vector.match_replace(left[r % 2][:], top[:, eight], now[:], -1.0))
                    now = left[r % 2]
            chain.wait()
            nc.vector.tensor_copy(top_at_f[:], top_at[:]).then_inc(chosen, 1)
            dve.wait_ge(lists_turned, 1)
            chain.link(nc.vector.tensor_copy(weight[:], x_turn[0][:, 0, 0:EXPERTS]))
            chain.link(nc.vector.tensor_copy(token[:], x_turn[0][:, 1, 0:EXPERTS]))
            nc.vector.tensor_copy(token_next[:], token[:, 0:1]).then_inc(indices_next, 1)
            for u in range(2):
                x_part(0, u)

            def body(e, last):
                for p in range(UNITS):
                    k = p + AHEAD
                    if k < UNITS:
                        split_low(e, k)
                    elif not last:
                        split_low(e + 1, k - UNITS)
                    if p == 6:
                        dve.wait_ge(y_free, e + 1)
                        if not last:
                            nc.vector.memset(idle[:, 0:1], 0.0)
                            nc.vector.tensor_copy(token_next[:], token[:, bass.ds(e + 1, 1)]).then_inc(indices_next, 1)
                            dve.wait_ge(indices_next, e + 2)
                        nc.vector.memset(idle[:, 1:2], 0.0)
                        nc.vector.tensor_copy(weight_now[:], weight[:, bass.ds(e, 1)])
                        nc.vector.tensor_copy(token_now[:], token[:, bass.ds(e, 1)]).then_inc(indices_now, 1)
                    for i in range(TILES):
                        if p == place["up", i] + 1:
                            dve.wait_ge(silu_done, TILES * e + i + 1)
                            nc.vector.tensor_tensor(act_sb[:, i % 2], silu[:, i % 2], pre[i % 2][:, 1, :], ALU.mult
                                                    ).then_inc(act_done, 1)
                        if p == (place["up", i + 1] if i < TILES - 1 else place["down", i]):
                            dve.wait_ge(act_high, TILES * e + i + 1)
                            nc.vector.tensor_tensor(actT[1][:], turn[:], actT[0][:], ALU.subtract
                                                    ).then_inc(act_split, 1)
                if not last:
                    for u in range(2):
                        x_part(e + 1, u)

            loop(dve, body)

        @block.tensor
        def _(pe):
            pe.sem_inc(unit_done, PARTS)
            pe.wait_ge(chosen, 1)
            nc.tensor.transpose(x_turn[0][:, 0, 0:EXPERTS], top[:], ident[0:EXPERTS, 0:EXPERTS])
            nc.tensor.transpose(x_turn[0][:, 1, 0:EXPERTS], top_at_f[:], ident[0:EXPERTS, 0:EXPERTS]
                                ).then_inc(lists_turned, 1)

            def turn_x(e):
                pe.wait_ge(gathered, 16 * e + 16)
                for u in range(2):
                    for c in range(4):
                        kc = 4 * u + c
                        last = nc.tensor.transpose(x_turn[u][:, c, :], xg[:, kc * P:(kc + 1) * P], ident)
                    last.then_inc(x_turned, 1)

            pe.wait_ge(indices_next, 1)
            turn_x(0)

            def turn_act(e, i):
                pe.wait_ge(act_done, 2 + TILES * e + i + 1)
                pe.wait_ge(act_split, TILES * e + i + 1)
                for c in range(2):
                    last = nc.tensor.transpose(turn[:, c, :], act_sb[:, i % 2, c * P:(c + 1) * P], ident)
                last.then_inc(act_turned, 1)

            def body(e, last):
                for k, (kind, i) in enumerate(order):
                    w = part[k % PARTS]
                    if kind == "down":
                        if i == TILES - 1:
                            turn_act(e, i)
                            if not last:
                                turn_x(e + 1)
                        pe.wait_ge(w_split, UNITS * e + k + 1)
                        pe.wait_ge(act_split, 1 + TILES * e + i + 1)
                        if i == 0:
                            pe.wait_ge(y_taken, e + 1)
                        for j in range(2):
                            for half in range(2):
                                for xi, wi in ((0, 0), (0, 1), (1, 0)):
                                    ins = nc.tensor.matmul(
                                        y_ps[:, half, :], actT[xi][:, j, :],
                                        w[wi][:, j * D + 512 * half:j * D + 512 * half + 512],
                                        start=(i, j, xi, wi) == (0, 0, 0, 0),
                                        stop=(i, j, xi, wi) == (TILES - 1, 1, 1, 0))
                    else:
                        pe.wait_ge(w_split, UNITS * e + k + 1)
                        if kind == "gate":
                            if i == 0:
                                pe.wait_ge(x_split, 2 * e + 2)
                            pe.wait_ge(act_done, TILES * e + (i + 1 if i else 2))
                        ins = product(nc, pre[i % 2][:, 0 if kind == "gate" else 1, :], xgT, w,
                                      lambda a, kc: a[:, kc, :], lambda a, kc: a[:, kc * FT:(kc + 1) * FT])
                    ins.then_inc(unit_done, 1)
                    if kind == "gate" and i:
                        turn_act(e, i - 1)

            loop(pe, body)


def normalize_output(nc, sems, x_in, x_mid, norm_final, cst, out):
    with ExitStack() as ctx:
        sb = lambda n, s, d=F32: ctx.enter_context(nc.sbuf_tensor(f"f_{n}", s, d))
        sem = lambda n: sems.enter_context(nc.semaphore(f"f_{n}"))
        x_sb = sb("x", [P, NT, D])
        y_sb = sb("y", [P, NT, D])
        gain_row = sb("gain_row", [P, D])
        stat = sb("stat", [P, 5, NT])
        gain_in = sem("gain_in")
        squared = sem("squared")
        meaned = sem("meaned")
        rooted = sem("rooted")
        normed = sem("normed")
        dve_chain = sem("dve_chain")
        stored = sem("stored")
        with nc.Block() as block:
            @block.sync
            def _(sp):
                for t in range(NT):
                    sp.dma_start(x_sb[:, t, :], x_mid[t * P:(t + 1) * P, :]).then_inc(x_in[t], 16)
                    if t == 0:
                        sp.dma_start(gain_row[:], norm_final.unsqueeze(0).to_broadcast([P, D])).then_inc(gain_in, 16)
                for t in range(NT):
                    sp.wait_ge(normed, t + 1)
                    sp.dma_start(out[0, t * P:(t + 1) * P, :], y_sb[:, t, :]).then_inc(stored, 16)
                sp.wait_ge(stored, 16 * NT)

            @block.scalar
            def _(act):
                for t in range(NT):
                    act.wait_ge(x_in[t], 32)
                    nc.scalar.activation(y_sb[:, t, :], x_sb[:, t, :], ACT.Square,
                                         accum_out=stat[:, 0, t:t + 1]).then_inc(squared, 1)
                    act.wait_ge(meaned, t + 1)
                    nc.scalar.activation(stat[:, 1, t:t + 1], stat[:, 3, t:t + 1], ACT.Sqrt).then_inc(rooted, 1)

            @block.vector
            def _(dve):
                chain = Chain(dve, dve_chain)
                dve.wait_ge(gain_in, 16)
                for t in range(NT):
                    dve.wait_ge(squared, t + 1)
                    nc.vector.tensor_scalar(stat[:, 3, t:t + 1], stat[:, 0, t:t + 1], 1.0 / D, EPS,
                                            ALU.mult, ALU.add).then_inc(meaned, 1)
                    dve.wait_ge(rooted, t + 1)
                    inverse_root(nc, chain, stat[:, 2, t:t + 1], stat[:, 1, t:t + 1],
                                 stat[:, 3, t:t + 1], stat[:, 4, t:t + 1])
                    nc.vector.scalar_tensor_tensor(out=y_sb[:, t, :], in0=x_sb[:, t, :], scalar=stat[:, 2, t:t + 1],
                                                   in1=gain_row[:], op0=ALU.mult, op1=ALU.mult).then_inc(normed, 1)


def build_encoder(nc, x, positions, consts, norm_mix, w_in, decay_fwd, decay_bwd, ret_norm, gate_w_fwd, gate_b_fwd,
                  gate_w_bwd, gate_b_bwd, gla_norm, w_branch_ret, w_branch_gla, w_out, norm_ffn, w_router,
                  w_gate, w_up, w_down, norm_final, out):
    dram = lambda n, s: nc.dram_tensor(n, s, F32, kind="Internal").ap()
    ret_T, gla_T = dram("ret_T", (2 * HEADS, P, SEQ)), dram("gla_T", (2 * HEADS, P, SEQ))
    gates = dram("gates", (SEQ, 2 * D))
    x_mid, h_mid = dram("x_mid", (SEQ, D)), dram("h_mid", (SEQ, D))
    with ExitStack() as sems, nc.sbuf_tensor("cst", [P, N_CONST], F32) as cst:
        x_in = [sems.enter_context(nc.semaphore(f"x_in{t}")) for t in range(NT)]
        with nc.sbuf_tensor("hT_high", [P, KC, SEQ], F32R) as h_high, nc.sbuf_tensor("hT_low", [P, KC, SEQ], F32R) as h_low:
            hT = (h_high, h_low)
            normalize_input(nc, sems, x_in, x, norm_mix, consts, cst, hT)
            heads(nc, sems, "ret", w_in, (decay_fwd, decay_bwd), ret_norm, positions, None, None, cst, hT, ret_T, gates)
            heads(nc, sems, "gla", w_in, None, gla_norm, None, (gate_w_fwd, gate_w_bwd), (gate_b_fwd, gate_b_bwd),
                  cst, hT, gla_T, gates)
        with nc.sbuf_tensor("affinity", [EXPERTS, SEQ], F32) as affinity:
            merge_and_route(nc, sems, x, ret_T, gla_T, gates, (w_branch_ret, w_branch_gla), w_out, norm_ffn, w_router, cst,
                            affinity, x_mid, h_mid)
            experts(nc, sems, affinity, cst, x_mid, h_mid, w_gate, w_up, w_down)
        normalize_output(nc, sems, x_in, x_mid, norm_final, cst, out)


_INS = ["x", "positions", "consts", "norm_mix", "w_in", "ret_decay_fwd", "ret_decay_bwd", "ret_norm", "gla_gate_w_fwd",
        "gla_gate_b_fwd", "gla_gate_w_bwd", "gla_gate_b_bwd", "gla_norm", "w_branch_ret", "w_branch_gla", "w_out",
        "norm_ffn", "w_router", "w_gate", "w_up", "w_down", "norm_final"]


def kernel(**inputs):
    import concourse.bacc as _bacc
    from concourse.bass_utils import run_bass_kernel_spmd as _run

    nc = _bacc.Bacc("TRN2", target_bir_lowering=False, num_devices=1)
    arrays, args = {}, []
    for name in _INS:
        a = make_constants() if name == "consts" else np.asarray(inputs[name])
        if name in ("norm_mix", "ret_norm", "gla_norm"):
            a = a.reshape(KC, P).T
        a = np.ascontiguousarray(a)
        arrays[f"in_{name}_dram"] = a
        args.append(nc.dram_tensor(f"in_{name}_dram", a.shape, mybir.dt.from_np(a.dtype), kind="ExternalInput").ap())
    out = nc.dram_tensor("out_dram", (1, SEQ, D), F32, kind="ExternalOutput").ap()
    build_encoder(nc, *args, out)
    r = _run(nc, [arrays], core_ids=[0])
    return r.results[0]["out_dram"]
```

```python
from contextlib import ExitStack

import numpy as np

import concourse.bass as bass
from concourse import mybir

ALU = mybir.AluOpType
ACT = mybir.ActivationFunctionType
F32 = mybir.dt.float32
F32R = mybir.dt.float32r
I32 = mybir.dt.int32
U32 = mybir.dt.uint32
AX_X = mybir.AxisListType.X

P = 128
SEQ = 1024
D = 1024
NT = SEQ // P
KC = D // P
HEADS = 4
DK = 128
DV = 256
RANK = 16
EXPERTS = 16
D_FF = 2816
CAPACITY = 2 * SEQ // EXPERTS
EPS = 1e-6
QK_SCALE = DK ** -0.5
GATE_NORMALIZER = 16.0
COLS = 256

RET_Q, RET_K, RET_V, RET_G = 0, 512, 1024, 2048
GLA_Q, GLA_K, GLA_V, GLA_G = 3072, 3584, 4096, 5120
GATE_A, GATE_LOGITS = 6144, 6176

C_IDENT, C_ROT, C_AHEAD, C_BEHIND = 0, 128, 256, 384
C_ROW, C_UPTO, C_FROM, C_AFTER = 512, 768, 896, 1024
C_INV_FREQ, C_COL, C_EPS, C_CHUNK = 1152, 1153, 1155, 1156
N_CONST = 1160


def make_constants():
    c = np.zeros((P, N_CONST), np.float32)
    j, i = np.arange(P)[:, None], np.arange(P)[None, :]
    c[:, C_IDENT:C_IDENT + P] = i == j
    half = DK // 2
    c[:, C_ROT:C_ROT + P] = np.where(j == i + half, -1.0, 0.0) + np.where(j == i - half, 1.0, 0.0)
    c[:, C_AHEAD:C_AHEAD + P] = np.maximum(i - j, 0)
    c[:, C_BEHIND:C_BEHIND + P] = np.maximum(j - i, 0)
    c[:, C_ROW:C_ROW + P] = i + 1
    c[:, C_ROW + P:C_ROW + 2 * P] = P - i
    c[:, C_UPTO:C_UPTO + P] = j <= i
    c[:, C_FROM:C_FROM + P] = j >= i
    c[:, C_AFTER:C_AFTER + P] = j > i
    freq = np.float32(10000.0) ** (-np.arange(0, DK, 2, dtype=np.float32) / np.float32(DK))
    c[:, C_INV_FREQ] = np.tile(freq, 2)
    c[:, C_COL] = P - 1 - np.arange(P)
    c[:, C_COL + 1] = np.arange(P)
    c[:, C_EPS] = EPS
    c[:, C_CHUNK] = P
    return c


class Chain:

    def __init__(self, eng, sem):
        self.eng, self.sem, self.base, self.n = eng, sem, 0, 0

    def start(self, base=0):
        self.base, self.n = base, 0

    def mark(self, ins):
        self.n += 1
        ins.then_inc(self.sem, 1)

    def wait(self):
        self.eng.wait_ge(self.sem, self.base + self.n)

    def link(self, ins):
        self.mark(ins)
        self.wait()


def inverse_root(nc, chain, out, root, square, scratch):
    chain.link(nc.vector.reciprocal(out, root))
    chain.link(nc.vector.tensor_tensor(scratch, out, out, ALU.mult))
    chain.link(nc.vector.tensor_tensor(scratch, scratch, square, ALU.mult))
    chain.link(nc.vector.tensor_scalar(scratch, scratch, -0.5, 1.5, ALU.mult, ALU.add))
    chain.link(nc.vector.tensor_tensor(out, out, scratch, ALU.mult))


def product(nc, out, x, w, x_at, w_at, chunks=KC, start=True, stop=True):
    for kc in range(chunks):
        for xi, wi in ((0, 0), (0, 1), (1, 0)):
            last = nc.tensor.matmul(out, x_at(x[xi], kc), w_at(w[wi], kc),
                                    start=start and kc == 0 and (xi, wi) == (0, 0),
                                    stop=stop and kc == chunks - 1 and (xi, wi) == (1, 0))
    return last


def normalize_input(nc, sems, x_in, x, norm_mix, consts, cst, hT):
    with ExitStack() as ctx:
        sb = lambda n, s, d=F32: ctx.enter_context(nc.sbuf_tensor(n, s, d))
        sem = lambda n: sems.enter_context(nc.semaphore(n))
        x_sb = sb("n1_x", [P, NT, D])
        xn = sb("n1_xn", [P, NT, D])
        gain = sb("n1_gain", [P, KC])
        stat = sb("n1_stat", [P, 5, NT])
        val = sb("n1_val", [P, 2, 4, P])
        tp = [ctx.enter_context(nc.psum_tensor(f"n1_tp{b}", [P, 4, P], F32)) for b in range(2)]
        small_in = sem("n1_small_in")
        squared = sem("n1_squared")
        rooted = sem("n1_rooted")
        meaned = sem("n1_meaned")
        dve_chain = sem("n1_dve_chain")
        normed = sem("n1_normed")
        transposed = sem("n1_transposed")
        scaled = sem("n1_scaled")
        high = sem("n1_high")
        low = sem("n1_low")
        ident = cst[:, C_IDENT:C_IDENT + P]
        with nc.Block() as block:
            @block.sync
            def _(sp):
                sp.dma_start(x_sb[:, 0, :], x[0, 0:P, :]).then_inc(x_in[0], 16)
                sp.dma_start(cst[:], consts).then_inc(small_in, 16)
                sp.dma_start(gain[:], norm_mix).then_inc(small_in, 16)
                for t in range(1, NT):
                    sp.dma_start(x_sb[:, t, :], x[0, t * P:(t + 1) * P, :]).then_inc(x_in[t], 16)

            @block.scalar
            def _(act):
                def split_high(u):
                    act.wait_ge(scaled, u + 1)
                    t, c0 = u // 2, 4 * (u % 2)
                    nc.scalar.activation(hT[0][:, c0:c0 + 4, t * P:(t + 1) * P], val[:, u % 2],
                                         ACT.Copy).then_inc(high, 1)

                act.wait_ge(small_in, 32)
                for t in range(NT):
                    act.wait_ge(x_in[t], 16)
                    nc.scalar.activation(xn[:, t, :], x_sb[:, t, :], ACT.Square,
                                         accum_out=stat[:, 0, t:t + 1]).then_inc(squared, 1)
                    act.wait_ge(meaned, t + 1)
                    nc.scalar.activation(stat[:, 1, t:t + 1], stat[:, 3, t:t + 1], ACT.Sqrt).then_inc(rooted, 1)
                    for half in range(2) if t else ():
                        split_high(2 * (t - 1) + half)
                for half in range(2):
                    split_high(2 * (NT - 1) + half)

            @block.vector
            def _(dve):
                def split_low(u):
                    t, c0 = u // 2, 4 * (u % 2)
                    at = (slice(None), slice(c0, c0 + 4), slice(t * P, (t + 1) * P))
                    dve.wait_ge(high, u + 1)
                    nc.vector.tensor_tensor(hT[1][at], val[:, u % 2], hT[0][at], ALU.subtract).then_inc(low, 1)

                def scale(u):
                    c0 = 4 * (u % 2)
                    dve.wait_ge(transposed, u + 1)
                    if u >= 2:
                        dve.wait_ge(low, u - 1)
                    nc.vector.tensor_tensor(val[:, u % 2], tp[u % 2][:],
                                            gain[:, c0:c0 + 4].unsqueeze(2).to_broadcast([P, 4, P]),
                                            ALU.mult).then_inc(scaled, 1)

                chain = Chain(dve, dve_chain)
                dve.wait_ge(small_in, 32)
                for t in range(NT + 1):
                    if t < NT:
                        dve.wait_ge(squared, t + 1)
                        nc.vector.tensor_scalar(stat[:, 3, t:t + 1], stat[:, 0, t:t + 1], 1.0 / D, EPS,
                                                ALU.mult, ALU.add).then_inc(meaned, 1)
                        dve.wait_ge(rooted, t + 1)
                        inverse_root(nc, chain, stat[:, 2, t:t + 1], stat[:, 1, t:t + 1],
                                     stat[:, 3, t:t + 1], stat[:, 4, t:t + 1])
                        nc.vector.tensor_scalar(xn[:, t, :], x_sb[:, t, :], stat[:, 2, t:t + 1], None,
                                                ALU.mult).then_inc(normed, 1)
                    if t:
                        for u in (2 * t - 2, 2 * t - 1):
                            scale(u)
                        for u in (2 * t - 2, 2 * t - 1):
                            split_low(u)

            @block.tensor
            def _(pe):
                pe.wait_ge(small_in, 32)
                for u in range(2 * NT):
                    t = u // 2
                    pe.wait_ge(normed, t + 1)
                    if u >= 2:
                        pe.wait_ge(scaled, u - 1)
                    for c in range(4):
                        kc = 4 * (u % 2) + c
                        last = nc.tensor.transpose(tp[u % 2][:, c, :], xn[:, t, kc * P:(kc + 1) * P], ident)
                    last.then_inc(transposed, 1)


def heads(nc, sems, branch, w_in, decay, gain_cols, positions, gate_w, gate_b, cst, hT, out_T, gates):
    ret = branch == "ret"
    q0, k0, v0, g0 = (RET_Q, RET_K, RET_V, RET_G) if ret else (GLA_Q, GLA_K, GLA_V, GLA_G)
    m0 = GATE_LOGITS + (0 if ret else D)
    m_out = 0 if ret else D
    kinds = (("turn", 4), ("keys", 2), ("state", NT - 1), ("score", 2), ("flip", 4)) if ret else \
        (("gate", 4), ("cum", 4), ("keys", 4), ("state", NT - 1), ("score", 4), ("flip", 4))
    units = [(kind, i) for kind, n in kinds for i in range(n)]
    order = {u: n for n, u in enumerate(units)}
    n_units = len(units)
    uses = ((n_units + 1) // 2, n_units // 2)
    A, B, C, DD = 0, 1, 2, 3
    T_LOAD = (32, 16, 16, 16)
    n_chain = 6 + 4 + NT * 2 if ret else 0

    with ExitStack() as ctx:
        sb = lambda n, s, d=F32: ctx.enter_context(nc.sbuf_tensor(f"{branch}_{n}", s, d))
        sem = lambda n: sems.enter_context(nc.semaphore(f"{branch}_{n}"))
        psum = lambda n, s: ctx.enter_context(nc.psum_tensor(f"{branch}_{n}", s, F32))
        w_raw = sb("w_raw", [P, KC, COLS])
        w_part = [[sb(f"w_part{i}{k}", [P, KC, COLS], F32R) for k in range(2)] for i in range(2)]
        qk_raw = sb("qk_raw", [P, 2, SEQ])
        o_n = qk_raw[:].rearrange("p w n -> p (w n)").rearrange("p (n e) -> p n e", e=DV)
        v_sb = sb("v", [P, NT, DV])
        g_sb = sb("g", [P, NT, DV])
        curve = sb("curve", [P, 2, SEQ])
        tmp = sb("tmp", [P, 2, SEQ])
        tmp_flat = tmp[:].rearrange("p w n -> p (w n)")
        n_dir = 1 if ret else 2
        qd = sb("qd", [P, n_dir, SEQ])
        kd = sb("kd", [P, n_dir, SEQ])
        qw = sb("qw", [P, 2, SEQ])
        kw = sb("kw", [P, NT, 2, DK])
        kw_flat = kw[:].rearrange("p n w d -> p (n w d)")
        states = sb("states", [P, 2, NT - 1, DV])
        probs = sb("probs", [P, NT, P])
        m_stage = sb("m_stage", [P, 2, 2, COLS])
        stats = sb("stats", [P, NT, 6])
        mv = sb("mv", [P, NT, 2])
        small = sb("small", [P, 4, NT])
        gain = sb("gain", [P, KC])
        head_cols = sb("head_cols", [P, 4])
        dec = sb("dec", [P, 2, HEADS if ret else NT])
        proj = [psum(f"proj{b}", [P, 512]) for b in range(2)]
        work = [psum(f"work{b}", [P, 512]) for b in range(2)]
        out = psum("out", [P, NT, DV])

        w_loaded = sem("w_loaded")
        w_high = sem("w_high")
        w_split = sem("w_split")
        proj_done = sem("proj_done")
        proj_taken = sem("proj_taken")
        work_done = sem("work_done")
        work_taken = [sem(f"work_taken{b}") for b in range(2)]
        roped = sem("roped")
        q_weighted = sem("q_weighted")
        state_f = sem("state_f")
        out_done = sem("out_done")
        squares_done = sem("squares_done")
        rooted = sem("rooted")
        out_normed = sem("out_normed")
        out_gated = sem("out_gated")
        stage_stored = sem("stage_stored")
        stage_free = sem("stage_free")
        m_stored = sem("m_stored")
        m_free = sem("m_free")
        dve_chain = sem("dve_chain")
        act_chain = sem("act_chain")
        small_in = sem("small_in")
        ident = cst[:, C_IDENT:C_IDENT + P]

        if ret:
            pos_i = sb("pos_i", [P, SEQ], I32)
            rows = sb("rows", [P, HEADS, 2, P])
            dists = sb("dists", [P, HEADS, P])
            cols = sb("cols", [P, HEADS, 2])
            lg = sb("lg", [P, 2, HEADS])
            lt = sb("lt", [P, 4, 2, HEADS])
            angles_done = sem("angles_done")
            tables_done = sem("tables_done")
            act_tables = sem("act_tables")
        else:
            low_rank = sb("low_rank", [64, SEQ])
            gate_all = cst[0:64, C_ROT:C_ROT + HEADS * DK]
            gate_head = sb("gate_head", [64, DK])
            wa_raw = states[:, 0, 0, :].rearrange("p (c n) -> p c n", c=KC)
            wa_part = [w_part[1][k][:, :, 0:32 + RANK] for k in range(2)]
            wa_high = sem("wa_high")
            wa_split = sem("wa_split")
            low_done = sem("low_done")
            low_taken = sem("low_taken")
            ones_set = sem("ones_set")
            gate_ready = sem("gate_ready")
            z_folded = sem("z_folded")
            decay_logs = sem("decay_logs")
            decays_ready = sem("decays_ready")
            diff_done = sem("diff_done")
            exp_done = sem("exp_done")
            keys_weighted = sem("keys_weighted")

        def taken_after(h, kind, i):
            n = order[(kind, i)]
            return n % 2, uses[n % 2] * h + n // 2 + 2

        def wait_taken(eng, h, kind, i):
            b, count = taken_after(h, kind, i)
            eng.wait_ge(work_taken[b], count)

        def wait_work(eng, h, kind, i):
            eng.wait_ge(work_done, n_units * h + order[(kind, i)] + 1)

        def bank(kind, i):
            return work[order[(kind, i)] % 2]

        def took(ins, kind, i):
            ins.then_inc(work_taken[order[(kind, i)] % 2], 1)

        def proj_unit(tile, i):
            return 4 * tile + i

        def wait_proj(eng, h, tile, i):
            eng.wait_ge(proj_done, 16 * h + proj_unit(tile, i) + 1)

        block = ctx.enter_context(nc.Block())

        @block.sync
        def _(sp):
            w = w_in[0].rearrange("(c p) n -> p c n", p=P)

            def load(tile, h):
                if tile == A:
                    sp.dma_start(w_raw[:, :, 0:DK], w[:, :, bass.ds(h * DK + q0, DK)]).then_inc(w_loaded, 16)
                    sp.dma_start(w_raw[:, :, DK:2 * DK], w[:, :, bass.ds(h * DK + k0, DK)]).then_inc(w_loaded, 16)
                else:
                    c0 = {B: v0, C: g0, DD: m0}[tile]
                    sp.dma_start(w_raw[:], w[:, :, bass.ds(h * COLS + c0, COLS)]).then_inc(w_loaded, 16)

            if ret:
                load(A, 0)
            sp.dma_start(gain[:], gain_cols).then_inc(small_in, 16)
            if ret:
                sp.dma_start(pos_i[:], positions.to_broadcast([P, SEQ])).then_inc(small_in, 16)
                for k in range(2):
                    sp.dma_start(lg[:, k, :], decay[k].to_broadcast([P, HEADS])).then_inc(small_in, 16)
            else:
                with nc.allow_non_contiguous_dma(reason="128-byte rows"):
                    sp.dma_start(wa_raw, w[:, :, GATE_A:GATE_A + 2 * RANK]).then_inc(small_in, 16)
                for k in range(2):
                    sp.dma_start(gate_all[32 * k:32 * k + RANK, :], gate_w[k][0]).then_inc(small_in, 16)
                    sp.dma_start(gate_all[32 * k + RANK:32 * k + RANK + 1, :], gate_b[k]).then_inc(small_in, 16)
                load(A, 0)
            with sp.Fori(0, HEADS) as h:
                for n, tile in enumerate((B, C, DD, A)):
                    sp.wait_ge(w_split, 4 * h + n + 1)
                    load(tile, h + 1 if tile == A else h)

        @block.gpsimd
        def _(pool):
            pool.sem_inc(stage_free, 1)
            pool.sem_inc(m_free, 2)
            with pool.Fori(0, HEADS) as h:
                def store_gates(i):
                    pool.wait_ge(proj_taken, 16 * h + proj_unit(DD, i) + 1 + 2)
                    pool.dma_start(gates.rearrange("(t p) n -> p t n", p=P)[
                        :, 2 * i:2 * i + 2, bass.ds(h * COLS + m_out, COLS)], m_stage[:, i % 2]
                        ).then_inc(m_stored, 16)
                    pool.wait_ge(m_stored, 64 * h + 16 * (i + 1))
                    pool.sem_inc(m_free, 1)
                for i in range(4):
                    store_gates(i)
                for i in range(4):
                    wait_taken(pool, h, "flip", i)
                    pool.dma_start(out_T[bass.ds(2 * h + i % 2, 1), :, (i // 2) * 512:(i // 2) * 512 + 512]
                                   .rearrange("a p n -> p (a n)"),
                                   tmp_flat[:, i * 512:(i + 1) * 512]).then_inc(stage_stored, 16)
                pool.wait_ge(stage_stored, 64 * h + 64)
                pool.sem_inc(stage_free, 1)

        @block.scalar
        def _(act):
            act.sem_inc(proj_taken, 2)
            for b in range(2):
                act.sem_inc(work_taken[b], 1)
            chain = Chain(act, act_chain)

            def split_high(n, tile, at, loaded):
                act.wait_ge(w_loaded, loaded)
                nc.scalar.activation(w_part[at][0][:], w_raw[:], ACT.Copy).then_inc(w_high, 1)

            if not ret:
                act.wait_ge(small_in, 96)
                for k in range(2):
                    nc.scalar.activation(wa_part[0][:, :, 32 * k:32 * k + RANK], wa_raw[:, :, RANK * k:RANK * (k + 1)],
                                         ACT.Copy).then_inc(wa_high, 1)
                nc.scalar.activation(wa_part[0][:, :, RANK:32], ident.rearrange("p (c n) -> p c n", c=KC), ACT.Copy,
                                     scale=0.0).then_inc(wa_high, 1)
            split_high(0, A, 0, 32)
            if ret:
                act.wait_ge(small_in, 64)
                chain.link(nc.scalar.activation(lt[:, 0], lg[:], ACT.Abs))
                chain.link(nc.scalar.activation(lt[:, 0], lt[:, 0], ACT.Exp, scale=-1.0))
                nc.scalar.activation(lt[:, 0], lt[:, 0], ACT.Ln, bias=1.0).then_inc(act_tables, 1)
                act.wait_ge(tables_done, 1)
                for h in range(HEADS):
                    for k in range(2):
                        s = lt[:, 3, k, h:h + 1]
                        nc.scalar.activation(rows[:, h, k, :], cst[:, C_ROW + k * P:C_ROW + (k + 1) * P],
                                             ACT.Exp, scale=s)
                        nc.scalar.activation(cols[:, h, k:k + 1], cst[:, C_COL + k:C_COL + k + 1],
                                             ACT.Exp, scale=s)
                        nc.scalar.activation(dec[:, k, h:h + 1], cst[:, C_CHUNK:C_CHUNK + 1],
                                             ACT.Exp, scale=s)
                nc.scalar.activation(dists[:], dists[:], ACT.Exp).then_inc(act_tables, 1)
                act.wait_ge(angles_done, 1)
                nc.scalar.activation(curve[:], curve[:], ACT.Sin).then_inc(act_tables, 1)
            else:
                act.wait_ge(ones_set, 1)
                for half in range(2):
                    act.wait_ge(low_done, half + 1)
                    for k in range(2):
                        nc.scalar.activation(low_rank[32 * k:32 * k + RANK, half * 512:half * 512 + 512],
                                             proj[half][32 * k:32 * k + RANK, :], ACT.Copy).then_inc(low_taken, 1)

            chain_base = chain.n
            with act.Fori(0, HEADS) as h:
                n_act = 0 if ret else 2
                chain.start(chain_base + n_act * h)
                loaded = 32 + sum(T_LOAD) * h

                def split_next(tile):
                    n = (tile + 1) % 4
                    count = loaded + sum((T_LOAD[B], T_LOAD[C], T_LOAD[DD], T_LOAD[A])[:tile + 1])
                    act.wait_ge(w_loaded, count)
                    nc.scalar.activation(w_part[n % 2][0][:], w_raw[:], ACT.Copy).then_inc(w_high, 1)

                def evacuate(tile, i):
                    wait_proj(act, h, tile, i)
                    src = proj[i % 2][:]
                    if tile == A:
                        ins = nc.scalar.activation(qk_raw[:, i // 2, (i % 2) * 512:(i % 2) * 512 + 512], src,
                                                   ACT.Copy, scale=QK_SCALE if i < 2 else 1.0)
                    elif tile == B:
                        ins = nc.scalar.activation(v_sb[:, 2 * i:2 * i + 2, :],
                                                   src.rearrange("p (t n) -> p t n", t=2), ACT.Copy)
                    elif tile == C:
                        ins = nc.scalar.activation(g_sb[:, 2 * i:2 * i + 2, :],
                                                   src.rearrange("p (t n) -> p t n", t=2), ACT.Silu)
                    else:
                        act.wait_ge(m_free, 4 * h + i + 1)
                        ins = nc.scalar.activation(m_stage[:, i % 2],
                                                   src.rearrange("p (t n) -> p t n", t=2), ACT.Sigmoid)
                    ins.then_inc(proj_taken, 1)

                if not ret:
                    nc.scalar.activation(gate_head[0:RANK + 1, :], gate_all[0:RANK + 1, bass.ds(h * DK, DK)], ACT.Copy)
                    nc.scalar.activation(gate_head[32:32 + RANK + 1, :],
                                         gate_all[32:32 + RANK + 1, bass.ds(h * DK, DK)],
                                         ACT.Copy).then_inc(gate_ready, 1)
                evacuate(A, 0)
                split_next(A)
                for i in range(1, 4):
                    evacuate(A, i)
                if not ret:
                    act.wait_ge(stage_free, h + 1)
                    for i in range(4):
                        wait_work(act, h, "gate", i)
                        nc.scalar.activation(tmp_flat[:, i * 512:i * 512 + 512], bank("gate", i)[:],
                                             ACT.Abs).then_inc(z_folded, 1)
                    act.wait_ge(z_folded, 4 * h + 4)
                    chain.link(nc.scalar.activation(tmp_flat, tmp_flat, ACT.Exp, scale=-1.0))
                    chain.link(nc.scalar.activation(tmp_flat, tmp_flat, ACT.Ln, bias=1.0))
                evacuate(B, 0)
                split_next(B)
                for i in range(1, 4):
                    evacuate(B, i)
                if not ret:
                    for i in range(4):
                        wait_work(act, h, "cum", i)
                        took(nc.scalar.activation(curve[:, i // 2, (i % 2) * 512:(i % 2) * 512 + 512],
                                                  bank("cum", i)[:], ACT.Copy), "cum", i)
                evacuate(C, 0)
                nc.scalar.activation(head_cols[:, 0:2], gain[:, bass.ds(2 * h, 2)], ACT.Copy)
                if ret:
                    nc.scalar.activation(head_cols[:, 2:4], cols[:, bass.ds(h, 1), :].rearrange("p h k -> p (h k)"),
                                         ACT.Copy)
                split_next(C)
                if not ret:
                    for k in range(2):
                        act.wait_ge(diff_done, 4 * h + k + 1)
                        nc.scalar.activation(qd[:, k, :], tmp[:, k, :], ACT.Exp)
                        nc.scalar.activation(kd[:, k, :], tmp[:, k, :], ACT.Exp, scale=-1.0).then_inc(exp_done, 1)
                    evacuate(C, 1)
                    for k in range(2):
                        nc.scalar.activation(qw[:, k, :], curve[:, k, :], ACT.Exp)
                        last = P - 1 if k == 0 else 0
                        nc.scalar.activation(dec[:, k, :], curve[:, k, :].rearrange("p (n i) -> p n i", i=P)[:, :, last],
                                             ACT.Exp)
                        act.wait_ge(diff_done, 4 * h + 2 + k + 1)
                        nc.scalar.activation(tmp[:, k, :], tmp[:, k, :], ACT.Exp).then_inc(exp_done, 1)
                    for i in range(2, 4):
                        evacuate(C, i)
                else:
                    for i in range(1, 4):
                        evacuate(C, i)
                    for i in range(2):
                        wait_work(act, h, "keys", i)
                        src = bank("keys", i)[:].rearrange("p (n d) -> p n d", d=DK)
                        for k in range(2):
                            ins = nc.scalar.activation(kw[:, 4 * i:4 * i + 4, k, :], src, ACT.Copy,
                                                       scale=head_cols[:, 2 + k:3 + k])
                        took(ins, "keys", i)
                evacuate(DD, 0)
                split_next(DD)
                evacuate(DD, 1)
                act.wait_ge(squares_done, h + 1)
                nc.scalar.activation(small[:, 1, :], small[:, 0, :], ACT.Sqrt).then_inc(rooted, 1)
                evacuate(DD, 2)
                evacuate(DD, 3)
                for i in range(4):
                    wait_work(act, h, "flip", i)
                    took(nc.scalar.activation(tmp_flat[:, i * 512:i * 512 + 512], bank("flip", i)[:], ACT.Copy,
                                              scale=head_cols[:, i % 2:i % 2 + 1]), "flip", i)
                assert chain.n == n_act

        @block.vector
        def _(dve):
            chain = Chain(dve, dve_chain)

            def split_low(n_total, at):
                dve.wait_ge(w_high, n_total)
                nc.vector.tensor_tensor(w_part[at][1][:], w_raw[:], w_part[at][0][:], ALU.subtract
                                        ).then_inc(w_split, 1)

            if not ret:
                nc.vector.memset(low_rank[0:64, :], 1.0).then_inc(ones_set, 1)
                for k in range(2):
                    at = (slice(None), slice(None), slice(32 * k, 32 * k + RANK))
                    dve.wait_ge(wa_high, k + 1)
                    nc.vector.tensor_tensor(wa_part[1][at], wa_raw[:, :, RANK * k:RANK * (k + 1)], wa_part[0][at],
                                            ALU.subtract).then_inc(wa_split, 1)
                dve.wait_ge(wa_high, 3)
                zeros = wa_part[0][:, :, RANK:32]
                nc.vector.tensor_tensor(wa_part[1][:, :, RANK:32], zeros, zeros, ALU.subtract).then_inc(wa_split, 1)
            split_low(1, 0)
            if ret:
                dve.wait_ge(small_in, 64)
                chain.link(nc.vector.tensor_scalar(lt[:, 1], lg[:], 0.0, None, ALU.min))
                dve.wait_ge(act_tables, 1)
                chain.link(nc.vector.tensor_tensor(lt[:, 3], lt[:, 1], lt[:, 0], ALU.subtract))
                for h in range(HEADS):
                    chain.link(nc.vector.tensor_scalar(dists[:, h, :], cst[:, C_AHEAD:C_AHEAD + P],
                                                       lt[:, 3, 0, h:h + 1], None, ALU.mult))
                    ins = nc.vector.scalar_tensor_tensor(out=dists[:, h, :], in0=cst[:, C_BEHIND:C_BEHIND + P],
                                                         scalar=lt[:, 3, 1, h:h + 1], in1=dists[:, h, :],
                                                         op0=ALU.mult, op1=ALU.add)
                ins.then_inc(tables_done, 1)
                ang, turns = curve[:, 1, :], tmp[:, 0, :]
                chain.link(nc.vector.tensor_copy(ang, pos_i[:]))
                chain.link(nc.vector.tensor_scalar(ang, ang, cst[:, C_INV_FREQ:C_INV_FREQ + 1], None, ALU.mult))
                magic = 1.5 * 2.0 ** 23
                chain.link(nc.vector.tensor_scalar(turns, ang, 1.0 / (2 * np.pi), magic, ALU.mult, ALU.add))
                chain.link(nc.vector.tensor_scalar(turns, turns, magic, None, ALU.subtract))
                first = 6.28125
                second = 253.0 * 2.0 ** -17
                third = 2 * np.pi - first - second
                for part in (first, second, third):
                    chain.link(nc.vector.scalar_tensor_tensor(out=ang, in0=turns, scalar=-part, in1=ang,
                                                              op0=ALU.mult, op1=ALU.add))
                cosine, over = curve[:, 0, :], tmp[:, 1, :]
                chain.link(nc.vector.tensor_scalar(cosine, ang, np.pi / 2, None, ALU.add))
                chain.link(nc.vector.tensor_scalar(over, cosine, np.pi, -2 * np.pi, ALU.is_gt, ALU.mult))
                chain.link(nc.vector.tensor_tensor(cosine, cosine, over, ALU.add))
                bound = float(np.nextafter(np.float32(np.pi), np.float32(0)))
                nc.vector.tensor_scalar(curve[:], curve[:], bound, -bound, ALU.min, ALU.max).then_inc(angles_done, 1)
                dve.wait_ge(act_tables, 3)

            chain_base = chain.n
            per = (4 + NT + 1 + 1 + 5 if ret else 4 + NT + 1 + 2 + 5)
            with dve.Fori(0, HEADS) as h:
                chain.start(chain_base + per * h)

                def split_next(tile):
                    split_low(4 * h + tile + 2, (tile + 1) % 2)

                split_next(A)
                if ret:
                    split_next(B)
                    dve.wait_ge(stage_free, h + 1)
                    for i in range(4):
                        w, half = i // 2, slice((i % 2) * 512, (i % 2) * 512 + 512)
                        wait_work(dve, h, "turn", i)
                        took(nc.vector.tensor_tensor(tmp[:, w, half], bank("turn", i)[:], curve[:, 1, half],
                                                     ALU.mult), "turn", i)
                        dst = (qd, kd)[w][:, 0, half]
                        chain.link(nc.vector.tensor_tensor(dst, qk_raw[:, w, half], curve[:, 0, half], ALU.mult))
                        nc.vector.tensor_tensor(dst, dst, tmp[:, w, half], ALU.add).then_inc(roped, 1)
                    split_next(C)
                    dve.wait_ge(roped, 4 * h + 4)
                    for k in range(2):
                        ins = nc.vector.tensor_tensor(
                            qw[:, k, :].rearrange("p (n i) -> p n i", i=P),
                            qd[:, 0, :].rearrange("p (n i) -> p n i", i=P),
                            rows[:, bass.ds(h, 1), k, :].to_broadcast([P, NT, P]), ALU.mult)
                    ins.then_inc(q_weighted, 1)
                else:
                    for i in range(4):
                        dve.wait_ge(z_folded, 4 * h + i + 1)
                        took(nc.vector.tensor_scalar(kw_flat[:, i * 512:i * 512 + 512], bank("gate", i)[:], 0.0,
                                                     1.0 / GATE_NORMALIZER, ALU.min, ALU.mult), "gate", i)
                    wait_taken(dve, h, "gate", 3)
                    wait_taken(dve, h, "gate", 2)
                    dve.wait_ge(act_chain, 2 * h + 2)
                    nc.vector.scalar_tensor_tensor(out=tmp_flat, in0=tmp_flat, scalar=-1.0 / GATE_NORMALIZER,
                                                   in1=kw_flat, op0=ALU.mult, op1=ALU.add).then_inc(decay_logs, 1)
                    split_next(B)

                    def cum(k):
                        return curve[:, k, :].rearrange("p (n i) -> p n i", i=P)

                    def diff(k):
                        return tmp[:, k, :].rearrange("p (n i) -> p n i", i=P)

                    for k in range(2):
                        wait_taken(dve, h, "cum", 2 * k)
                        wait_taken(dve, h, "cum", 2 * k + 1)
                        if k == 0:
                            wait_work(dve, h, "cum", 3)
                        mid = P // 2 if k == 0 else P // 2 - 1
                        nc.vector.tensor_tensor(diff(k), cum(k), cum(k)[:, :, mid:mid + 1].to_broadcast([P, NT, P]),
                                                ALU.subtract).then_inc(diff_done, 1)
                    split_next(C)
                    for k in range(2):
                        dve.wait_ge(exp_done, 4 * h + k + 1)
                        last = P - 1 if k == 0 else 0
                        nc.vector.tensor_tensor(diff(k), cum(k)[:, :, last:last + 1].to_broadcast([P, NT, P]), cum(k),
                                                ALU.subtract).then_inc(diff_done, 1)
                        nc.vector.tensor_tensor(qd[:, k, :], qd[:, k, :], qk_raw[:, 0, :], ALU.mult)
                        nc.vector.tensor_tensor(kd[:, k, :], kd[:, k, :], qk_raw[:, 1, :], ALU.mult)
                    for k in range(2):
                        dve.wait_ge(exp_done, 4 * h + 2 + k + 1)
                        nc.vector.tensor_tensor(tmp[:, k, :], tmp[:, k, :], qk_raw[:, 1, :], ALU.mult)
                        ins = nc.vector.tensor_tensor(qw[:, k, :], qw[:, k, :], qk_raw[:, 0, :], ALU.mult)
                        ins.then_inc(keys_weighted, 1)
                    for i in range(4):
                        wait_work(dve, h, "keys", i)
                        took(nc.vector.tensor_copy(kw_flat[:, i * 512:i * 512 + 512], bank("keys", i)[:]), "keys", i)
                for i in range(NT - 1):
                    wait_work(dve, h, "state", i)
                    src = bank("state", i)
                    back = NT - 2 - i
                    if i == 0:
                        nc.vector.tensor_copy(states[:, 0, 0, :], src[:, 0:DV]).then_inc(state_f, 1)
                        took(nc.vector.tensor_copy(states[:, 1, back, :], src[:, DV:2 * DV]), "state", i)
                        continue
                    wait_taken(dve, h, "state", i - 1)
                    d_f = dec[:, 0, bass.ds(h, 1)] if ret else dec[:, 0, i:i + 1]
                    d_b = dec[:, 1, bass.ds(h, 1)] if ret else dec[:, 1, back + 1:back + 2]
                    nc.vector.scalar_tensor_tensor(out=states[:, 0, i, :], in0=states[:, 0, i - 1, :], scalar=d_f,
                                                   in1=src[:, 0:DV], op0=ALU.mult, op1=ALU.add).then_inc(state_f, 1)
                    took(nc.vector.scalar_tensor_tensor(out=states[:, 1, back, :], in0=states[:, 1, back + 1, :],
                                                        scalar=d_b, in1=src[:, DV:2 * DV], op0=ALU.mult,
                                                        op1=ALU.add), "state", i)
                split_next(DD)
                if ret:
                    for i in range(2):
                        wait_work(dve, h, "score", i)
                        took(nc.vector.tensor_tensor(probs[:, 4 * i:4 * i + 4, :],
                                                     bank("score", i)[:].rearrange("p (n i) -> p n i", i=P),
                                                     dists[:, bass.ds(h, 1), :].to_broadcast([P, 4, P]), ALU.mult),
                             "score", i)
                else:
                    for i in range(4):
                        wait_work(dve, h, "score", i)
                        nc.vector.memset(small[:, 3, i:i + 1], 0.0)
                        src = bank("score", i)[:].rearrange("p (n w i) -> p n w i", n=2, w=2)
                        for k, c in enumerate((C_UPTO, C_AFTER)):
                            mask = cst[:, c:c + P].bitcast(U32).unsqueeze(1).to_broadcast([P, 2, P])
                            ins = nc.vector.copy_predicated(probs[:, 2 * i:2 * i + 2, :], mask, src[:, :, k, :])
                            if k == 0:
                                chain.link(ins)
                                nc.vector.memset(small[:, 3, 4 + i:5 + i], 0.0)
                        took(ins, "score", i)
                for n in range(NT):
                    if n % 2 == 0:
                        dve.wait_ge(out_done, NT * h + n + 2)
                    chain.wait()
                    chain.mark(nc.vector.bn_stats(stats[:, n, :], out[:, n, :]))
                    if n:
                        nc.vector.bn_aggr(mv[:, n - 1, :], stats[:, n - 1, :])
                chain.wait()
                nc.vector.memset(small[:, 3, :], 0.0)
                chain.link(nc.vector.bn_aggr(mv[:, NT - 1, :], stats[:, NT - 1, :]))
                if ret:
                    chain.mark(nc.vector.tensor_scalar(small[:, 0, :], mv[:, :, 1], EPS, None, ALU.add))
                    chain.wait()
                    nc.vector.tensor_copy(small[:, 3, :], mv[:, :, 0]).then_inc(squares_done, 1)
                else:
                    chain.link(nc.vector.tensor_tensor(small[:, 0, :], mv[:, :, 0], mv[:, :, 0], ALU.mult))
                    chain.link(nc.vector.tensor_tensor(small[:, 0, :], small[:, 0, :], mv[:, :, 1], ALU.add))
                    nc.vector.tensor_scalar(small[:, 0, :], small[:, 0, :], EPS, None, ALU.add
                                            ).then_inc(squares_done, 1)
                dve.wait_ge(rooted, h + 1)
                inverse_root(nc, chain, small[:, 2, :], small[:, 1, :], small[:, 0, :], small[:, 1, :])
                for n in range(NT):
                    if ret:
                        ins = nc.vector.tensor_scalar(o_n[:, n, :], out[:, n, :], small[:, 3, n:n + 1],
                                                      small[:, 2, n:n + 1], ALU.subtract, ALU.mult)
                    else:
                        ins = nc.vector.tensor_scalar(o_n[:, n, :], out[:, n, :], small[:, 2, n:n + 1], None, ALU.mult)
                    if n % 4 == 3:
                        ins.then_inc(out_normed, 1)
                for half in range(2):
                    dve.wait_ge(out_normed, 2 * h + half + 1)
                    at = slice(4 * half, 4 * half + 4)
                    nc.vector.tensor_tensor(o_n[:, at, :], o_n[:, at, :], g_sb[:, at, :], ALU.mult
                                            ).then_inc(out_gated, 1)
                assert chain.n == per, (chain.n, per)

        @block.tensor
        def _(pe):
            if not ret:
                pe.wait_ge(wa_split, 3)
                for half in range(2):
                    last = product(nc, proj[half][0:32 + RANK, :], wa_part, hT, lambda x, kc: x[:, kc, :],
                                   lambda y, kc: y[:, kc, half * 512:half * 512 + 512])
                    last.then_inc(low_done, 1)
                pe.wait_ge(low_taken, 4)

            with pe.Fori(0, HEADS) as h:
                def project(tile, i):
                    if i == 0:
                        pe.wait_ge(w_split, 4 * h + tile + 1)
                    pe.wait_ge(proj_taken, 16 * h + proj_unit(tile, i) + 1)
                    w = w_part[tile % 2]
                    if tile == A:
                        c0 = DK * (i // 2)
                        last = product(nc, proj[i % 2][:], w, hT, lambda x, kc: x[:, kc, c0:c0 + DK],
                                       lambda y, kc: y[:, kc, (i % 2) * 512:(i % 2) * 512 + 512])
                    else:
                        for t in range(2 * i, 2 * i + 2):
                            last = product(nc, proj[i % 2][:, (t % 2) * COLS:(t % 2) * COLS + COLS], hT, w,
                                           lambda x, kc: x[:, kc, t * P:(t + 1) * P], lambda y, kc: y[:, kc, :])
                    last.then_inc(proj_done, 1)

                def begin(kind, i):
                    n = order[(kind, i)]
                    pe.wait_ge(work_taken[n % 2], uses[n % 2] * h + n // 2 + 1)
                    return bank(kind, i)

                for i in range(4):
                    project(A, i)
                if not ret:
                    pe.wait_ge(gate_ready, h + 1)
                    for i in range(4):
                        dst = begin("gate", i)
                        k = i % 2
                        for n in range(4):
                            t = 4 * (i // 2) + n
                            last = nc.tensor.matmul(dst[:, n * DK:(n + 1) * DK],
                                                    low_rank[32 * k:32 * k + RANK + 1, t * P:(t + 1) * P],
                                                    gate_head[32 * k:32 * k + RANK + 1, :], start=True, stop=True)
                        last.then_inc(work_done, 1)
                for i in range(4):
                    project(B, i)
                if ret:
                    for i in range(4):
                        dst = begin("turn", i)
                        pe.wait_ge(proj_taken, 16 * h + i + 1 + 2)
                        nc.tensor.matmul(dst[:], cst[:, C_ROT:C_ROT + P],
                                         qk_raw[:, i // 2, (i % 2) * 512:(i % 2) * 512 + 512],
                                         start=True, stop=True).then_inc(work_done, 1)
                else:
                    pe.wait_ge(decay_logs, h + 1)
                    for i in range(4):
                        dst = begin("cum", i)
                        k = i // 2
                        tri = cst[:, (C_UPTO, C_FROM)[k]:(C_UPTO, C_FROM)[k] + P]
                        for n in range(4):
                            c = 4 * (i % 2) + n
                            at = 512 * (2 * (c // 4) + k) + DK * (c % 4)
                            last = nc.tensor.matmul(dst[:, n * P:(n + 1) * P], tmp_flat[:, at:at + DK], tri,
                                                    start=True, stop=True)
                        last.then_inc(work_done, 1)
                for i in range(4):
                    project(C, i)
                if ret:
                    for i in range(2):
                        dst = begin("keys", i)
                        pe.wait_ge(roped, 4 * h + 2 + i + 1)
                        for n in range(4):
                            c = 4 * i + n
                            last = nc.tensor.transpose(dst[:, n * P:(n + 1) * P], kd[:, 0, c * P:(c + 1) * P], ident)
                        last.then_inc(work_done, 1)
                    for i in range(2):
                        project(DD, i)
                else:
                    for i in range(2):
                        project(DD, i)
                    pe.wait_ge(keys_weighted, 2 * h + 2)
                    for i in range(4):
                        dst = begin("keys", i)
                        for n in range(2):
                            for k in range(2):
                                c = 2 * i + n
                                last = nc.tensor.transpose(dst[:, (2 * n + k) * DK:(2 * n + k + 1) * DK],
                                                           tmp[:, k, c * P:(c + 1) * P], ident)
                        last.then_inc(work_done, 1)
                for i in range(NT - 1):
                    dst = begin("state", i)
                    if i == 0:
                        pe.wait_ge(proj_taken, 16 * h + proj_unit(B, 3) + 1 + 2)
                        for j in range(2 if ret else 4):
                            wait_taken(pe, h, "keys", j)
                    for k, c in ((0, i), (1, NT - 1 - i)):
                        last = nc.tensor.matmul(dst[:, k * DV:(k + 1) * DV], kw[:, c, k, :], v_sb[:, c, :],
                                                start=True, stop=True)
                    last.then_inc(work_done, 1)
                if ret:
                    for i in range(2):
                        dst = begin("score", i)
                        for n in range(4):
                            c = slice((4 * i + n) * P, (4 * i + n + 1) * P)
                            last = nc.tensor.matmul(dst[:, n * P:(n + 1) * P], kd[:, 0, c], qd[:, 0, c],
                                                    start=True, stop=True)
                        last.then_inc(work_done, 1)
                    pe.wait_ge(q_weighted, h + 1)
                else:
                    for i in range(4):
                        dst = begin("score", i)
                        for n in range(2):
                            for k in range(2):
                                c = slice((2 * i + n) * P, (2 * i + n + 1) * P)
                                last = nc.tensor.matmul(dst[:, (2 * n + k) * P:(2 * n + k + 1) * P], kd[:, k, c],
                                                        qd[:, k, c], start=True, stop=True)
                        last.then_inc(work_done, 1)
                wait_taken(pe, h, "state", NT - 2)
                for n in range(NT):
                    per_unit = 4 if ret else 2
                    if n % per_unit == 0:
                        wait_taken(pe, h, "score", n // per_unit)
                    c = slice(n * P, (n + 1) * P)
                    terms = [(probs[:, n, :], v_sb[:, n, :])]
                    if n > 0:
                        terms.append((qw[:, 0, c], states[:, 0, n - 1, :]))
                    if n < NT - 1:
                        terms.append((qw[:, 1, c], states[:, 1, n, :]))
                    for j, (x, y) in enumerate(terms):
                        last = nc.tensor.matmul(out[:, n, :], x, y, start=j == 0, stop=j == len(terms) - 1)
                    last.then_inc(out_done, 1)
                for i in range(2, 4):
                    project(DD, i)
                for i in range(4):
                    dst = begin("flip", i)
                    half, e = i // 2, i % 2
                    pe.wait_ge(out_gated, 2 * h + half + 1)
                    for n in range(4):
                        last = nc.tensor.transpose(dst[:, n * P:(n + 1) * P],
                                                   o_n[:, 4 * half + n, e * P:(e + 1) * P], ident)
                    last.then_inc(work_done, 1)


def merge_and_route(nc, sems, x, ret_T, gla_T, gates, w_branches, w_out, norm_ffn, w_router, cst, affinity, x_mid,
                    h_mid):
    TILES, BLOCKS, TOK = 12, 4, 2 * P
    LAST = (3, 7, 11)
    with ExitStack() as ctx:
        sb = lambda n, s, d=F32: ctx.enter_context(nc.sbuf_tensor(f"m_{n}", s, d))
        sem = lambda n: sems.enter_context(nc.semaphore(f"m_{n}"))
        psum = lambda n, s: ctx.enter_context(nc.psum_tensor(f"m_{n}", s, F32))
        w_raw = sb("w_raw", [P, KC, COLS])
        w_part = [[sb(f"w_part{i}{k}", [P, KC, COLS], F32R) for k in range(2)] for i in range(2)]
        x_raw = sb("x_raw", [P, 2, KC, TOK])
        xT = [sb(f"xT{k}", [P, KC, SEQ], F32R) for k in range(2)]
        merged = sb("merged", [P, NT, D])
        side = sb("side", [P, 4, 2, COLS])
        prod = sb("prod", [P, 2, 2, COLS])
        h2 = sb("h2", [P, 4, D])
        h2T = sb("h2T", [P, 2, KC, P])
        gain_row = sb("gain_row", [P, D])
        router = sb("router", [P, KC, EXPERTS])
        stat = sb("stat", [P, 5, NT])
        logit = sb("logit", [P, NT, EXPERTS])
        peak = sb("peak", [P, 3, NT])
        proj = [psum(f"proj{b}", [P, 512]) for b in range(2)]
        work = [psum(f"work{b}", [P, 4, P]) for b in range(2)]
        logits = psum("logits", [P, NT, EXPERTS])
        turned = [psum(f"turned{b}", [EXPERTS, 4, P]) for b in range(2)]

        w_loaded = sem("w_loaded")
        w_high = sem("w_high")
        w_split = sem("w_split")
        x_loaded = [sem(f"x_loaded{i}") for i in range(2)]
        x_high = sem("x_high")
        x_split = sem("x_split")
        side_in = [sem(f"side_in{i}") for i in range(4)]
        proj_done = sem("proj_done")
        proj_taken = sem("proj_taken")
        summed = sem("summed")
        merged_T = sem("merged_T")
        m_high = sem("m_high")
        m_low = sem("m_low")
        small_in = sem("small_in")
        squared = sem("squared")
        meaned = sem("meaned")
        rooted = sem("rooted")
        normed = sem("normed")
        h_turned = sem("h_turned")
        h_copied = sem("h_copied")
        logits_done = sem("logits_done")
        x_stored = sem("x_stored")
        h_stored = [sem(f"h_stored{i}") for i in range(4)]
        shifted = sem("shifted")
        exped = sem("exped")
        softmaxed = sem("softmaxed")
        aff_turned = sem("aff_turned")
        dve_chain = sem("dve_chain")
        ident = cst[:, C_IDENT:C_IDENT + P]
        block = ctx.enter_context(nc.Block())

        def unit(n, i):
            return BLOCKS * n + i + 1

        @block.sync
        def _(sp):
            def load_w(n):
                w = (*w_branches, w_out)[n // 4]
                c = n % 4
                sp.dma_start(w_raw[:], w[0].rearrange("(c p) n -> p c n", p=P)[:, :, c * COLS:(c + 1) * COLS]
                             ).then_inc(w_loaded, 16)

            def load_x(b):
                src = (ret_T, gla_T)[b // BLOCKS].rearrange("k p t -> p k t")
                if b >= 2:
                    sp.wait_ge(x_split, b - 1)
                t0 = (b % BLOCKS) * TOK
                sp.dma_start(x_raw[:, b % 2], src[:, :, t0:t0 + TOK]).then_inc(x_loaded[b % 2], 16)

            load_w(0)
            load_x(0)
            load_x(1)
            sp.dma_start(gain_row[:], norm_ffn.to_broadcast([P, D])).then_inc(small_in, 16)
            sp.dma_start(router[:], w_router[0].rearrange("(c p) n -> p c n", p=P)).then_inc(small_in, 16)
            for n in range(TILES - 1):
                sp.wait_ge(w_split, n + 1)
                load_w(n + 1)
                if n == 0:
                    load_x(2)
                    load_x(3)
                if n == 1:
                    load_x(4)
                    load_x(5)
                if n == LAST[0]:
                    load_x(6)
                    load_x(7)
            for t in range(NT):
                if t % 2 == 0:
                    sp.wait_ge(proj_taken, unit(LAST[2], t // 2))
                sp.dma_start(x_mid[t * P:(t + 1) * P, :], merged[:, t, :]).then_inc(x_stored, 16)
                sp.wait_ge(normed, t + 1)
                sp.dma_start(h_mid[t * P:(t + 1) * P, :], h2[:, t % 4]).then_inc(h_stored[t % 4], 16)
            sp.wait_ge(x_stored, 16 * NT)
            for i in range(4):
                sp.wait_ge(h_stored[i], 16 * (NT // 4))

        @block.gpsimd
        def _(pool):
            for n in range(TILES):
                for i in range(BLOCKS):
                    if n:
                        pool.wait_ge(proj_taken, unit(n - 1, i))
                    c0 = (n % 4) * COLS + (D if n // 4 == 1 else 0)
                    src = (gates if n < 8 else x[0]).rearrange("(t p) n -> p t n", p=P)
                    pool.dma_start(side[:, i], src[:, 2 * i:2 * i + 2, c0:c0 + COLS]).then_inc(side_in[i], 16)

        @block.scalar
        def _(act):
            def split_w(n):
                act.wait_ge(w_loaded, 16 * (n + 1))
                nc.scalar.activation(w_part[n % 2][0][:], w_raw[:], ACT.Copy).then_inc(w_high, 1)

            def split_x(b):
                act.wait_ge(x_loaded[b % 2], 16 * (b // 2 + 1))
                t0 = (b % BLOCKS) * TOK
                nc.scalar.activation(xT[0][:, :, t0:t0 + TOK], x_raw[:, b % 2], ACT.Copy).then_inc(x_high, 1)

            def split_merged(b):
                for f in range(4 * b, 4 * b + 4):
                    act.wait_ge(merged_T, f + 1)
                    t, c0 = f // 2, 4 * (f % 2)
                    nc.scalar.activation(xT[0][:, c0:c0 + 4, t * P:(t + 1) * P], work[f % 2][:], ACT.Copy
                                         ).then_inc(m_high, 1)

            def mean_squares(b):
                act.wait_ge(proj_taken, unit(LAST[2], b))
                for t in (2 * b, 2 * b + 1):
                    if t >= 4:
                        act.wait_ge(h_stored[t % 4], 16 * (t // 4))
                        act.wait_ge(h_turned, 2 * (t - 3))
                    nc.scalar.activation(h2[:, t % 4], merged[:, t, :], ACT.Square,
                                         accum_out=stat[:, 0, t:t + 1]).then_inc(squared, 1)
                act.wait_ge(meaned, b + 1)
                nc.scalar.activation(stat[:, 1, 2 * b:2 * b + 2], stat[:, 3, 2 * b:2 * b + 2], ACT.Sqrt
                                     ).then_inc(rooted, 1)

            def copy_h(b):
                for f in range(4 * b, 4 * b + 4):
                    t, half = f // 2, f % 2
                    act.wait_ge(h_turned, f + 1)
                    if t >= 2 and half == 0:
                        act.wait_ge(logits_done, t - 1)
                    nc.scalar.activation(h2T[:, t % 2, 4 * half:4 * half + 4, :], work[f % 2][:], ACT.Copy
                                         ).then_inc(h_copied, 1)

            split_w(0)
            for b in range(BLOCKS):
                split_x(b)
            for n in range(TILES):
                for i in range(BLOCKS):
                    act.wait_ge(proj_done, unit(n, i))
                    if n == LAST[0]:
                        split_x(BLOCKS + i)
                    if n == LAST[1] and i:
                        split_merged(i - 1)
                    if n == LAST[1] + 1 and i == 0:
                        split_merged(BLOCKS - 1)
                    if i == 0 and n + 1 < TILES:
                        split_w(n + 1)
                    if n == LAST[2]:
                        mean_squares(i)
                        if i:
                            copy_h(i - 1)
            copy_h(BLOCKS - 1)
            act.wait_ge(shifted, 1)
            nc.scalar.activation(logit[:], logit[:], ACT.Exp).then_inc(exped, 1)
            for b in range(2):
                act.wait_ge(aff_turned, b + 1)
                nc.scalar.activation(affinity[:, 512 * b:512 * b + 512].rearrange("e (t p) -> e t p", p=P),
                                     turned[b][:], ACT.Copy)

        @block.vector
        def _(dve):
            chain = Chain(dve, dve_chain)

            def split_w(n):
                dve.wait_ge(w_high, n + 1)
                nc.vector.tensor_tensor(w_part[n % 2][1][:], w_raw[:], w_part[n % 2][0][:], ALU.subtract
                                        ).then_inc(w_split, 1)

            def split_x(b):
                dve.wait_ge(x_high, b + 1)
                at = (slice(None), slice(None), slice((b % BLOCKS) * TOK, (b % BLOCKS + 1) * TOK))
                nc.vector.tensor_tensor(xT[1][at], x_raw[:, b % 2], xT[0][at], ALU.subtract).then_inc(x_split, 1)

            def split_merged(b):
                for f in range(4 * b, 4 * b + 4):
                    dve.wait_ge(m_high, f + 1)
                    at = (slice(None), slice(4 * (f % 2), 4 * (f % 2) + 4), slice(f // 2 * P, (f // 2 + 1) * P))
                    nc.vector.tensor_tensor(xT[1][at], work[f % 2][:], xT[0][at], ALU.subtract).then_inc(m_low, 1)

            def take(n, i):
                dve.wait_ge(proj_done, unit(n, i))
                dve.wait_ge(side_in[i], 16 * (n + 1))
                dst = merged[:, 2 * i:2 * i + 2, (n % 4) * COLS:(n % 4 + 1) * COLS]
                src = proj[i % 2][:].rearrange("p (t n) -> p t n", t=2)
                if n // 4 == 0:
                    nc.vector.tensor_tensor(dst, src, side[:, i], ALU.mult).then_inc(proj_taken, 1)
                elif n // 4 == 1:
                    nc.vector.tensor_tensor(prod[:, i % 2], src, side[:, i], ALU.mult).then_inc(proj_taken, 1)
                    dve.wait_ge(proj_taken, unit(n, i))
                    nc.vector.tensor_tensor(dst, dst, prod[:, i % 2], ALU.add).then_inc(summed, 1)
                else:
                    nc.vector.tensor_tensor(dst, src, side[:, i], ALU.add).then_inc(proj_taken, 1)

            def norm(b):
                at = slice(2 * b, 2 * b + 2)
                dve.wait_ge(squared, 2 * b + 2)
                nc.vector.tensor_scalar(stat[:, 3, at], stat[:, 0, at], 1.0 / D, EPS, ALU.mult, ALU.add
                                        ).then_inc(meaned, 1)
                dve.wait_ge(rooted, b + 1)
                inverse_root(nc, chain, stat[:, 2, at], stat[:, 1, at], stat[:, 3, at], stat[:, 4, at])
                for t in (2 * b, 2 * b + 1):
                    nc.vector.scalar_tensor_tensor(out=h2[:, t % 4], in0=merged[:, t, :], scalar=stat[:, 2, t:t + 1],
                                                   in1=gain_row[:], op0=ALU.mult, op1=ALU.mult).then_inc(normed, 1)

            split_w(0)
            for b in range(BLOCKS):
                split_x(b)
            dve.wait_ge(small_in, 32)
            for n in range(TILES):
                for i in range(BLOCKS):
                    take(n, i)
                    if n == LAST[0]:
                        split_x(BLOCKS + i)
                    if n == LAST[1] and i:
                        split_merged(i - 1)
                    if n == LAST[1] + 1 and i == 0:
                        split_merged(BLOCKS - 1)
                    if i == 0 and n + 1 < TILES:
                        split_w(n + 1)
                    if n == LAST[2]:
                        norm(i)
            dve.wait_ge(logits_done, NT)
            wide = lambda a: a.unsqueeze(2).to_broadcast([P, NT, EXPERTS])
            chain.link(nc.vector.tensor_reduce(peak[:, 0, :], logits[:], AX_X, ALU.max))
            nc.vector.tensor_tensor(logit[:], logits[:], wide(peak[:, 0, :]), ALU.subtract).then_inc(shifted, 1)
            dve.wait_ge(exped, 1)
            chain.link(nc.vector.tensor_reduce(peak[:, 1, :], logit[:], AX_X, ALU.add))
            chain.link(nc.vector.reciprocal(peak[:, 2, :], peak[:, 1, :]))
            nc.vector.tensor_tensor(logit[:], logit[:], wide(peak[:, 2, :]), ALU.mult).then_inc(softmaxed, 1)

        @block.tensor
        def _(pe):
            def turn_merged(b):
                pe.wait_ge(summed, 4 * 3 + b + 1)
                for f in range(4 * b, 4 * b + 4):
                    if f >= 2:
                        pe.wait_ge(m_low, f - 1)
                    for c in range(4):
                        kc = 4 * (f % 2) + c
                        last = nc.tensor.transpose(work[f % 2][:, c, :], merged[:, f // 2, kc * P:(kc + 1) * P], ident)
                    last.then_inc(merged_T, 1)

            def turn_h(b):
                for f in range(4 * b, 4 * b + 4):
                    t, half = f // 2, f % 2
                    pe.wait_ge(normed, t + 1)
                    if f >= 2:
                        pe.wait_ge(h_copied, f - 1)
                    for c in range(4):
                        kc = 4 * half + c
                        last = nc.tensor.transpose(work[f % 2][:, c, :], h2[:, t % 4, kc * P:(kc + 1) * P], ident)
                    last.then_inc(h_turned, 1)
                    if half:
                        route(t)

            def route(t):
                pe.wait_ge(h_copied, 2 * t + 2)
                for kc in range(KC):
                    last = nc.tensor.matmul(logits[:, t, :], h2T[:, t % 2, kc, :], router[:, kc, :],
                                            start=kc == 0, stop=kc == KC - 1)
                last.then_inc(logits_done, 1)

            for n in range(TILES):
                for i in range(BLOCKS):
                    if n % 4 == 0 and n < 8:
                        pe.wait_ge(x_split, n + i + 1)
                    if n == 8:
                        pe.wait_ge(m_low, 4 * i + 4)
                    pe.wait_ge(w_split, n + 1)
                    if 4 * n + i >= 2:
                        pe.wait_ge(proj_taken, 4 * n + i - 1)
                    for t in range(2 * i, 2 * i + 2):
                        last = product(nc, proj[i % 2][:, (t % 2) * COLS:(t % 2) * COLS + COLS], xT, w_part[n % 2],
                                       lambda a, kc: a[:, kc, t * P:(t + 1) * P], lambda a, kc: a[:, kc, :])
                    last.then_inc(proj_done, 1)
                    if n == LAST[1] and i:
                        turn_merged(i - 1)
                    if n == 8 and i == 0:
                        turn_merged(BLOCKS - 1)
                    if n == LAST[2] and i:
                        if i == 1:
                            pe.wait_ge(small_in, 32)
                        turn_h(i - 1)
            turn_h(BLOCKS - 1)
            pe.wait_ge(softmaxed, 1)
            for b in range(2):
                for c in range(4):
                    last = nc.tensor.transpose(turned[b][:, c, :], logit[:, 4 * b + c, :], ident)
                last.then_inc(aff_turned, 1)


def experts(nc, sems, affinity, cst, x_mid, h_mid, w_gate, w_up, w_down):
    FT = COLS
    TILES = D_FF // FT
    UNITS = 3 * TILES
    RAW, PARTS, AHEAD = 11, 3, 2
    assert UNITS % RAW == 0 and UNITS % PARTS == 0 and D_FF % FT == 0
    order = [("gate", 0), ("up", 0)]
    for i in range(1, TILES):
        order += [("gate", i), ("up", i), ("down", i - 1)]
    order.append(("down", TILES - 1))
    place = {u: k for k, u in enumerate(order)}
    ROUNDS = CAPACITY // 8
    HALVES = (slice(0, KC * FT // 2), slice(KC * FT // 2, KC * FT))

    with ExitStack() as ctx:
        sb = lambda n, s, d=F32: ctx.enter_context(nc.sbuf_tensor(f"e_{n}", s, d))
        sem = lambda n: sems.enter_context(nc.semaphore(f"e_{n}"))
        psum = lambda n, s: ctx.enter_context(nc.psum_tensor(f"e_{n}", s, F32))
        raw = [sb(f"raw{s}", [P, KC * FT]) for s in range(RAW)]
        part = [[sb(f"part{s}{k}", [P, KC * FT], F32R) for k in range(2)] for s in range(PARTS)]
        xg = sb("xg", [P, D])
        xgT = [sb(f"xgT{k}", [P, KC, P], F32R) for k in range(2)]
        silu = sb("silu", [P, 2, FT])
        act_sb = sb("act", [P, 2, FT])
        actT = [sb(f"actT{k}", [P, 2, P], F32R) for k in range(2)]
        y_sb = sb("y", [P, D])
        left = [sb(f"left{k}", [EXPERTS, SEQ]) for k in range(2)]
        top = sb("top", [EXPERTS, CAPACITY])
        top_at = sb("top_at", [EXPERTS, CAPACITY], U32)
        top_at_f = sb("top_at_f", [EXPERTS, CAPACITY])
        weight = sb("weight", [P, EXPERTS])
        token = sb("token", [P, EXPERTS], U32)
        weight_now = sb("weight_now", [P, 1])
        token_now = sb("token_now", [P, 1], U32)
        token_next = sb("token_next", [P, 1], U32)
        idle = sb("idle", [P, 2])
        pool_idle = sb("pool_idle", [P, 2])
        pre = [psum(f"pre{b}", [P, 2, FT]) for b in range(2)]
        turn = psum("turn", [P, 2, P])
        x_turn = [psum(f"x_turn{b}", [P, 4, P]) for b in range(2)]
        y_ps = psum("y_ps", [P, 2, 512])

        raw_in = [sem(f"raw_in{s}") for s in range(RAW)]
        w_high = sem("w_high")
        w_split = sem("w_split")
        unit_done = sem("unit_done")
        silu_done = sem("silu_done")
        act_done = sem("act_done")
        act_turned = sem("act_turned")
        act_high = sem("act_high")
        act_split = sem("act_split")
        gathered = sem("gathered")
        x_turned = sem("x_turned")
        x_high = sem("x_high")
        x_split = sem("x_split")
        y_taken = sem("y_taken")
        scattered = sem("scattered")
        y_free = sem("y_free")
        chosen = sem("chosen")
        lists_turned = sem("lists_turned")
        indices_next = sem("indices_next")
        indices_now = sem("indices_now")
        dve_chain = sem("dve_chain")
        carried = sem("carried")
        ident = cst[:, C_IDENT:C_IDENT + P]
        block = ctx.enter_context(nc.Block())

        def loop(eng, body):
            with eng.Fori(0, EXPERTS - 1) as e:
                body(e, False)
            body(EXPERTS - 1, True)

        @block.sync
        def _(sp):
            def load(e, k):
                kind, i = order[k]
                if kind == "down":
                    src = w_down[0][bass.ds(e, 1), i * FT:(i + 1) * FT, :].rearrange("e (j p) n -> p (e j) n", p=P)
                    dst = raw[k % RAW][:].rearrange("p (j n) -> p j n", j=2)
                else:
                    w = w_gate if kind == "gate" else w_up
                    src = w[0][bass.ds(e, 1), :, i * FT:(i + 1) * FT].rearrange("e (c p) n -> p (e c) n", p=P)
                    dst = raw[k % RAW][:].rearrange("p (c n) -> p c n", c=KC)
                sp.dma_start(dst, src).then_inc(raw_in[k % RAW], 16)

            for k in range(RAW):
                load(0, k)

            def body(e, last):
                for k in range(UNITS - RAW if last else UNITS):
                    sp.wait_ge(w_split, UNITS * e + k + 1)
                    load(e + (k + RAW) // UNITS, (k + RAW) % UNITS)

            loop(sp, body)

        @block.gpsimd
        def _(pool):
            pool.sem_inc(y_free, 1)

            def carry_wait(at):
                nc.gpsimd.tensor_tensor(pool_idle[:, at:at + 1], cst[:, C_EPS:C_EPS + 1], cst[:, C_EPS:C_EPS + 1],
                                        ALU.add).then_inc(carried, 1)

            def gather():
                pool.indirect_dma_start(xg[:], None, h_mid, bass.IndirectOffsetOnAxis(ap=token_next[:, 0:1], axis=0)
                                        ).then_inc(gathered, 16)

            pool.wait_ge(indices_next, 1)
            gather()

            def body(e, last):
                if not last:
                    pool.wait_ge(indices_next, e + 2)
                    pool.wait_ge(x_turned, 2 * e + 2)
                    carry_wait(0)
                    gather()
                pool.wait_ge(indices_now, e + 1)
                pool.wait_ge(y_taken, e + 2)
                pool.wait_ge(carried, 2 * e + (0 if last else 1))
                carry_wait(1)
                pool.indirect_dma_start(x_mid, bass.IndirectOffsetOnAxis(ap=token_now[:, 0:1], axis=0), y_sb[:], None,
                                        compute_op=ALU.add).then_inc(scattered, 16)
                pool.wait_ge(scattered, 16 * e + 16)
                pool.sem_inc(y_free, 1)

            loop(pool, body)

        @block.scalar
        def _(act):
            act.sem_inc(y_taken, 1)

            def split_high(e, k):
                n = UNITS * e + k
                act.wait_ge(raw_in[k % RAW], 16 * (UNITS // RAW) * e + 16 * (k // RAW + 1))
                act.wait_ge(unit_done, n + 1)
                for half in HALVES:
                    nc.scalar.activation(part[k % PARTS][0][:, half], raw[k % RAW][:, half], ACT.Copy
                                         ).then_inc(w_high, 1)

            def x_part(e, u):
                act.wait_ge(x_turned, 2 * e + u + 1)
                nc.scalar.activation(xgT[0][:, 4 * u:4 * u + 4, :], x_turn[u][:], ACT.Copy).then_inc(x_high, 1)

            for k in range(AHEAD):
                split_high(0, k)
            for u in range(2):
                x_part(0, u)

            def body(e, last):
                for p in range(UNITS):
                    for i in range(TILES):
                        if p == place["up", i] + 1:
                            act.wait_ge(unit_done, PARTS + UNITS * e + p)
                            nc.scalar.activation(silu[:, i % 2], pre[i % 2][:, 0, :], ACT.Silu).then_inc(silu_done, 1)
                        if p == (place["up", i + 1] if i < TILES - 1 else place["down", i]):
                            act.wait_ge(act_turned, TILES * e + i + 1)
                            nc.scalar.activation(actT[0][:], turn[:], ACT.Copy).then_inc(act_high, 1)
                    k = p + AHEAD
                    if k < UNITS:
                        split_high(e, k)
                    elif not last:
                        split_high(e + 1, k - UNITS)
                if not last:
                    for u in range(2):
                        x_part(e + 1, u)
                act.wait_ge(unit_done, PARTS + UNITS * e + UNITS)
                act.wait_ge(y_free, e + 1)
                act.wait_ge(indices_now, e + 1)
                for half in range(2):
                    ins = nc.scalar.activation(y_sb[:, 512 * half:512 * half + 512], y_ps[:, half, :], ACT.Copy,
                                               scale=weight_now[:, 0:1])
                ins.then_inc(y_taken, 1)

            loop(act, body)

        @block.vector
        def _(dve):
            chain = Chain(dve, dve_chain)
            dve.sem_inc(act_done, 2)
            dve.sem_inc(act_split, 1)

            def split_low(e, k):
                for n, half in enumerate(HALVES):
                    dve.wait_ge(w_high, 2 * UNITS * e + 2 * k + n + 1)
                    ins = nc.vector.tensor_tensor(part[k % PARTS][1][:, half], raw[k % RAW][:, half],
                                                  part[k % PARTS][0][:, half], ALU.subtract)
                ins.then_inc(w_split, 1)

            def x_part(e, u):
                dve.wait_ge(x_high, 2 * e + u + 1)
                nc.vector.tensor_tensor(xgT[1][:, 4 * u:4 * u + 4, :], x_turn[u][:], xgT[0][:, 4 * u:4 * u + 4, :],
                                        ALU.subtract).then_inc(x_split, 1)

            for k in range(AHEAD):
                split_low(0, k)
            now = affinity
            for r in range(ROUNDS):
                eight = slice(8 * r, 8 * r + 8)
                chain.link(nc.vector.max(top[:, eight], now[:]))
                chain.mark(nc.vector.max_index(top_at[:, eight], top[:, eight], now[:]))
                if r < ROUNDS - 1:
                    chain.link(nc.vector.match_replace(left[r % 2][:], top[:, eight], now[:], -1.0))
                    now = left[r % 2]
            chain.wait()
            nc.vector.tensor_copy(top_at_f[:], top_at[:]).then_inc(chosen, 1)
            dve.wait_ge(lists_turned, 1)
            chain.link(nc.vector.tensor_copy(weight[:], x_turn[0][:, 0, 0:EXPERTS]))
            chain.link(nc.vector.tensor_copy(token[:], x_turn[0][:, 1, 0:EXPERTS]))
            nc.vector.tensor_copy(token_next[:], token[:, 0:1]).then_inc(indices_next, 1)
            for u in range(2):
                x_part(0, u)

            def body(e, last):
                for p in range(UNITS):
                    for i in range(TILES):
                        if p == place["up", i] + 1:
                            dve.wait_ge(silu_done, TILES * e + i + 1)
                            nc.vector.tensor_tensor(act_sb[:, i % 2], silu[:, i % 2], pre[i % 2][:, 1, :], ALU.mult
                                                    ).then_inc(act_done, 1)
                        if p == (place["up", i + 1] if i < TILES - 1 else place["down", i]):
                            dve.wait_ge(act_high, TILES * e + i + 1)
                            nc.vector.tensor_tensor(actT[1][:], turn[:], actT[0][:], ALU.subtract
                                                    ).then_inc(act_split, 1)
                    k = p + AHEAD
                    if k < UNITS:
                        split_low(e, k)
                    elif not last:
                        split_low(e + 1, k - UNITS)
                    if p == 6:
                        dve.wait_ge(y_free, e + 1)
                        if not last:
                            nc.vector.memset(idle[:, 0:1], 0.0)
                            nc.vector.tensor_copy(token_next[:], token[:, bass.ds(e + 1, 1)]).then_inc(indices_next, 1)
                            dve.wait_ge(indices_next, e + 2)
                        nc.vector.memset(idle[:, 1:2], 0.0)
                        nc.vector.tensor_copy(weight_now[:], weight[:, bass.ds(e, 1)])
                        nc.vector.tensor_copy(token_now[:], token[:, bass.ds(e, 1)]).then_inc(indices_now, 1)
                if not last:
                    for u in range(2):
                        x_part(e + 1, u)

            loop(dve, body)

        @block.tensor
        def _(pe):
            pe.sem_inc(unit_done, PARTS)
            pe.wait_ge(chosen, 1)
            nc.tensor.transpose(x_turn[0][:, 0, 0:EXPERTS], top[:], ident[0:EXPERTS, 0:EXPERTS])
            nc.tensor.transpose(x_turn[0][:, 1, 0:EXPERTS], top_at_f[:], ident[0:EXPERTS, 0:EXPERTS]
                                ).then_inc(lists_turned, 1)

            def turn_x(e):
                pe.wait_ge(gathered, 16 * e + 16)
                for u in range(2):
                    for c in range(4):
                        kc = 4 * u + c
                        last = nc.tensor.transpose(x_turn[u][:, c, :], xg[:, kc * P:(kc + 1) * P], ident)
                    last.then_inc(x_turned, 1)

            pe.wait_ge(indices_next, 1)
            turn_x(0)

            def turn_act(e, i):
                pe.wait_ge(act_done, 2 + TILES * e + i + 1)
                pe.wait_ge(act_split, TILES * e + i + 1)
                for c in range(2):
                    last = nc.tensor.transpose(turn[:, c, :], act_sb[:, i % 2, c * P:(c + 1) * P], ident)
                last.then_inc(act_turned, 1)

            def body(e, last):
                for k, (kind, i) in enumerate(order):
                    w = part[k % PARTS]
                    if kind == "down":
                        if i == TILES - 1:
                            turn_act(e, i)
                            if not last:
                                turn_x(e + 1)
                        pe.wait_ge(w_split, UNITS * e + k + 1)
                        pe.wait_ge(act_split, 1 + TILES * e + i + 1)
                        if i == 0:
                            pe.wait_ge(y_taken, e + 1)
                        for j in range(2):
                            for half in range(2):
                                for xi, wi in ((0, 0), (0, 1), (1, 0)):
                                    ins = nc.tensor.matmul(
                                        y_ps[:, half, :], actT[xi][:, j, :],
                                        w[wi][:, j * D + 512 * half:j * D + 512 * half + 512],
                                        start=(i, j, xi, wi) == (0, 0, 0, 0),
                                        stop=(i, j, xi, wi) == (TILES - 1, 1, 1, 0))
                    else:
                        pe.wait_ge(w_split, UNITS * e + k + 1)
                        if kind == "gate":
                            if i == 0:
                                pe.wait_ge(x_split, 2 * e + 2)
                            pe.wait_ge(act_done, TILES * e + (i + 1 if i else 2))
                        ins = product(nc, pre[i % 2][:, 0 if kind == "gate" else 1, :], xgT, w,
                                      lambda a, kc: a[:, kc, :], lambda a, kc: a[:, kc * FT:(kc + 1) * FT])
                    ins.then_inc(unit_done, 1)
                    if kind == "gate" and i:
                        turn_act(e, i - 1)

            loop(pe, body)


def normalize_output(nc, sems, x_in, x_mid, norm_final, cst, out):
    with ExitStack() as ctx:
        sb = lambda n, s, d=F32: ctx.enter_context(nc.sbuf_tensor(f"f_{n}", s, d))
        sem = lambda n: sems.enter_context(nc.semaphore(f"f_{n}"))
        x_sb = sb("x", [P, NT, D])
        y_sb = sb("y", [P, NT, D])
        gain_row = sb("gain_row", [P, D])
        stat = sb("stat", [P, 5, NT])
        gain_in = sem("gain_in")
        squared = sem("squared")
        meaned = sem("meaned")
        rooted = sem("rooted")
        normed = sem("normed")
        dve_chain = sem("dve_chain")
        stored = sem("stored")
        with nc.Block() as block:
            @block.sync
            def _(sp):
                for t in range(NT):
                    sp.dma_start(x_sb[:, t, :], x_mid[t * P:(t + 1) * P, :]).then_inc(x_in[t], 16)
                    if t == 0:
                        sp.dma_start(gain_row[:], norm_final.unsqueeze(0).to_broadcast([P, D])).then_inc(gain_in, 16)
                for t in range(NT):
                    sp.wait_ge(normed, t + 1)
                    sp.dma_start(out[0, t * P:(t + 1) * P, :], y_sb[:, t, :]).then_inc(stored, 16)
                sp.wait_ge(stored, 16 * NT)

            @block.scalar
            def _(act):
                for t in range(NT):
                    act.wait_ge(x_in[t], 32)
                    nc.scalar.activation(y_sb[:, t, :], x_sb[:, t, :], ACT.Square,
                                         accum_out=stat[:, 0, t:t + 1]).then_inc(squared, 1)
                    act.wait_ge(meaned, t + 1)
                    nc.scalar.activation(stat[:, 1, t:t + 1], stat[:, 3, t:t + 1], ACT.Sqrt).then_inc(rooted, 1)

            @block.vector
            def _(dve):
                chain = Chain(dve, dve_chain)
                dve.wait_ge(gain_in, 16)
                for t in range(NT):
                    dve.wait_ge(squared, t + 1)
                    nc.vector.tensor_scalar(stat[:, 3, t:t + 1], stat[:, 0, t:t + 1], 1.0 / D, EPS,
                                            ALU.mult, ALU.add).then_inc(meaned, 1)
                    dve.wait_ge(rooted, t + 1)
                    inverse_root(nc, chain, stat[:, 2, t:t + 1], stat[:, 1, t:t + 1],
                                 stat[:, 3, t:t + 1], stat[:, 4, t:t + 1])
                    nc.vector.scalar_tensor_tensor(out=y_sb[:, t, :], in0=x_sb[:, t, :], scalar=stat[:, 2, t:t + 1],
                                                   in1=gain_row[:], op0=ALU.mult, op1=ALU.mult).then_inc(normed, 1)


def build_encoder(nc, x, positions, consts, norm_mix, w_in, decay_fwd, decay_bwd, ret_norm, gate_w_fwd, gate_b_fwd,
                  gate_w_bwd, gate_b_bwd, gla_norm, w_branch_ret, w_branch_gla, w_out, norm_ffn, w_router,
                  w_gate, w_up, w_down, norm_final, out):
    dram = lambda n, s: nc.dram_tensor(n, s, F32, kind="Internal").ap()
    ret_T, gla_T = dram("ret_T", (2 * HEADS, P, SEQ)), dram("gla_T", (2 * HEADS, P, SEQ))
    gates = dram("gates", (SEQ, 2 * D))
    x_mid, h_mid = dram("x_mid", (SEQ, D)), dram("h_mid", (SEQ, D))
    with ExitStack() as sems, nc.sbuf_tensor("cst", [P, N_CONST], F32) as cst:
        x_in = [sems.enter_context(nc.semaphore(f"x_in{t}")) for t in range(NT)]
        with nc.sbuf_tensor("hT_high", [P, KC, SEQ], F32R) as h_high, nc.sbuf_tensor("hT_low", [P, KC, SEQ], F32R) as h_low:
            hT = (h_high, h_low)
            normalize_input(nc, sems, x_in, x, norm_mix, consts, cst, hT)
            heads(nc, sems, "ret", w_in, (decay_fwd, decay_bwd), ret_norm, positions, None, None, cst, hT, ret_T, gates)
            heads(nc, sems, "gla", w_in, None, gla_norm, None, (gate_w_fwd, gate_w_bwd), (gate_b_fwd, gate_b_bwd),
                  cst, hT, gla_T, gates)
        with nc.sbuf_tensor("affinity", [EXPERTS, SEQ], F32) as affinity:
            merge_and_route(nc, sems, x, ret_T, gla_T, gates, (w_branch_ret, w_branch_gla), w_out, norm_ffn, w_router, cst,
                            affinity, x_mid, h_mid)
            experts(nc, sems, affinity, cst, x_mid, h_mid, w_gate, w_up, w_down)
        normalize_output(nc, sems, x_in, x_mid, norm_final, cst, out)


_INS = ["x", "positions", "consts", "norm_mix", "w_in", "ret_decay_fwd", "ret_decay_bwd", "ret_norm", "gla_gate_w_fwd",
        "gla_gate_b_fwd", "gla_gate_w_bwd", "gla_gate_b_bwd", "gla_norm", "w_branch_ret", "w_branch_gla", "w_out",
        "norm_ffn", "w_router", "w_gate", "w_up", "w_down", "norm_final"]


def kernel(**inputs):
    import concourse.bacc as _bacc
    from concourse.bass_utils import run_bass_kernel_spmd as _run

    nc = _bacc.Bacc("TRN2", target_bir_lowering=False, num_devices=1)
    arrays, args = {}, []
    for name in _INS:
        a = make_constants() if name == "consts" else np.asarray(inputs[name])
        if name in ("norm_mix", "ret_norm", "gla_norm"):
            a = a.reshape(KC, P).T
        a = np.ascontiguousarray(a)
        arrays[f"in_{name}_dram"] = a
        args.append(nc.dram_tensor(f"in_{name}_dram", a.shape, mybir.dt.from_np(a.dtype), kind="ExternalInput").ap())
    out = nc.dram_tensor("out_dram", (1, SEQ, D), F32, kind="ExternalOutput").ap()
    build_encoder(nc, *args, out)
    r = _run(nc, [arrays], core_ids=[0])
    return r.results[0]["out_dram"]
```
